# Optimizing a Trainium2 kernel written in Bass

```python
import math
import jax, jax.numpy as jnp
from jax import lax
import numpy as np
import jax
import jax.numpy as jnp

D_MODEL = 1024
BATCH = 1
SEQ = 512
DEPTH = 4

N_MIXERS = 3
EPS = 1e-6
N_GLA = (DEPTH + 2) // 3
N_SGU = (DEPTH + 1) // 3
N_FOX = DEPTH // 3

GLA_HEADS = 4
GLA_DK = D_MODEL // (2 * GLA_HEADS)
GLA_DV = D_MODEL // GLA_HEADS
GLA_KD = GLA_HEADS * GLA_DK
GLA_VD = GLA_HEADS * GLA_DV
GLA_RANK = 16
GLA_NORMALIZER = 16.0
GLA_CHUNK = 64
GLA_IN = 2 * GLA_KD + 2 * GLA_VD + GLA_RANK

SGU_WIDTH = D_MODEL
SGU_GROUPS = 4
SGU_GDIM = SGU_WIDTH // SGU_GROUPS
SGU_CHUNK = 128
SGU_IN = 3 * SGU_WIDTH

FOX_HEADS = 16
FOX_DH = 64
FOX_AD = FOX_HEADS * FOX_DH
FOX_BLOCK = 128
FOX_IN = 4 * FOX_AD + FOX_HEADS
FORGET_BIAS_INIT = 2.0


def rms_norm(x, g):
    xf = x.astype(jnp.float32)
    xf = xf * lax.rsqrt(jnp.mean(xf * xf, axis=-1, keepdims=True) + EPS)
    return xf.astype(x.dtype) * g

def layer_norm(x, g, b):
    xf = x.astype(jnp.float32)
    mu = jnp.mean(xf, axis=-1, keepdims=True)
    var = jnp.mean(jnp.square(xf - mu), axis=-1, keepdims=True)
    return ((xf - mu) * lax.rsqrt(var + EPS)).astype(x.dtype) * g + b

def gla_mixer(h, w_in, w_a2, b_a, g_head, w_out):
    B, S, _ = h.shape
    H, DK, DV, C = GLA_HEADS, GLA_DK, GLA_DV, GLA_CHUNK
    N = S // C
    q, k, v, z, a_low = jnp.split(h @ w_in, [GLA_KD, 2 * GLA_KD, 2 * GLA_KD + GLA_VD,
                                             2 * GLA_KD + 2 * GLA_VD], axis=-1)
    log_a = jax.nn.log_sigmoid((a_low @ w_a2 + b_a).astype(jnp.float32)) / GLA_NORMALIZER
    q = q.astype(jnp.float32) * (DK ** -0.5)

    def to_chunks(t, d):
        return t.astype(jnp.float32).reshape(B, N, C, H, d).transpose(1, 0, 3, 2, 4)

    qc, kc, vc, gc = to_chunks(q, DK), to_chunks(k, DK), to_chunks(v, DV), to_chunks(log_a, DK)
    causal = jnp.tril(jnp.ones((C, C), dtype=bool))

    def step(state, xs):
        qb, kb, vb, gb = xs
        b = jnp.cumsum(gb, axis=2)
        o_inter = jnp.einsum('bhik,bhkv->bhiv', qb * jnp.exp(b), state)
        diff = b[:, :, :, None, :] - b[:, :, None, :, :]
        decay = jnp.exp(jnp.where(causal[:, :, None], diff, -jnp.inf))
        attn = jnp.einsum('bhik,bhjk,bhijk->bhij', qb, kb, decay)
        o = o_inter + jnp.einsum('bhij,bhjv->bhiv', attn, vb)
        b_last = b[:, :, -1:, :]
        state = (jnp.exp(b_last[:, :, 0, :])[..., None] * state
                 + jnp.einsum('bhjk,bhjv->bhkv', kb * jnp.exp(b_last - b), vb))
        return state, o

    state0 = jnp.zeros((B, H, DK, DV), jnp.float32)
    _, o = lax.scan(step, state0, (qc, kc, vc, gc))
    o = o.transpose(1, 0, 3, 2, 4).reshape(B, S, H, DV)
    o = rms_norm(o, g_head).reshape(B, S, GLA_VD).astype(h.dtype)
    return (o * jax.nn.silu(z)) @ w_out

def sgu_mixer(h, w_in, ln_g, ln_b, w_s, b_s, w_out):
    B, S, _ = h.shape
    C, G, Dg = SGU_CHUNK, SGU_GROUPS, SGU_GDIM
    N = S // C
    u, v, z = jnp.split(h @ w_in, 3, axis=-1)
    u = jax.nn.gelu(u)
    v = layer_norm(jax.nn.gelu(v), ln_g, ln_b)
    w_causal = jnp.where(jnp.tril(jnp.ones((C, C), dtype=bool))[None], w_s, 0.0)
    vc = v.reshape(B, N, C, G, Dg)
    mixed = jnp.einsum('gts,bnsgd->bntgd', w_causal, vc) + b_s.T[None, None, :, :, None]
    sg = u * mixed.reshape(B, S, SGU_WIDTH)
    return (sg * jax.nn.silu(z)) @ w_out

def fox_mixer(h, w_in, b_f, g_q, g_k, w_out):
    B, S, _ = h.shape
    H, Dh, BLK = FOX_HEADS, FOX_DH, FOX_BLOCK
    q, k, v, z, f_logit = jnp.split(h @ w_in, [FOX_AD, 2 * FOX_AD, 3 * FOX_AD, 4 * FOX_AD], axis=-1)
    q = rms_norm(q.reshape(B, S, H, Dh), g_q).transpose(0, 2, 1, 3)
    k = rms_norm(k.reshape(B, S, H, Dh), g_k).transpose(0, 2, 1, 3)
    v = v.reshape(B, S, H, Dh).transpose(0, 2, 1, 3)
    log_f = jax.nn.log_sigmoid((f_logit + b_f).astype(jnp.float32))
    F = jnp.cumsum(log_f, axis=1).transpose(0, 2, 1)
    scale = Dh ** -0.5
    outs = []
    for i in range(S // BLK):
        lo, hi = i * BLK, (i + 1) * BLK
        s = jnp.einsum('bhqd,bhkd->bhqk', q[:, :, lo:hi], k[:, :, :hi]).astype(jnp.float32) * scale
        s = s + F[:, :, lo:hi, None] - F[:, :, None, :hi]
        causal = (lo + jnp.arange(BLK))[:, None] >= jnp.arange(hi)[None, :]
        p = jax.nn.softmax(jnp.where(causal, s, -jnp.inf), axis=-1).astype(v.dtype)
        outs.append(jnp.einsum('bhqk,bhkd->bhqd', p, v[:, :, :hi]))
    o = jnp.concatenate(outs, axis=2).transpose(0, 2, 1, 3).reshape(B, S, FOX_AD)
    return (o * jax.nn.silu(z)) @ w_out

def first_inputs(seed: int = 0) -> dict:
    key = jax.random.key(seed)
    ks = jax.random.split(key, 32)
    D = D_MODEL
    nrm = lambda k, shape, s: jax.random.normal(k, shape, jnp.float32) * s
    return {
        "x": nrm(ks[0], (BATCH, SEQ, D), 1.0),
        "c": nrm(ks[1], (BATCH, D), 1.0),
        "norm_pre_g": 1.0 + nrm(ks[2], (DEPTH, D), 0.1),
        "norm_post_g": 1.0 + nrm(ks[3], (DEPTH, D), 0.1),
        "w_mod": nrm(ks[4], (DEPTH, D, 3 * D), D ** -0.5),
        "b_mod": nrm(ks[5], (DEPTH, 3 * D), 0.01),
        "gla_w_in": nrm(ks[6], (N_GLA, D, GLA_IN), D ** -0.5),
        "gla_w_a2": nrm(ks[7], (N_GLA, GLA_RANK, GLA_KD), GLA_RANK ** -0.5),
        "gla_b_a": nrm(ks[8], (N_GLA, GLA_KD), 0.1),
        "gla_g_head": 1.0 + nrm(ks[9], (N_GLA, GLA_HEADS, GLA_DV), 0.1),
        "gla_w_out": nrm(ks[10], (N_GLA, GLA_VD, D), GLA_VD ** -0.5),
        "sgu_w_in": nrm(ks[11], (N_SGU, D, SGU_IN), D ** -0.5),
        "sgu_ln_g": 1.0 + nrm(ks[12], (N_SGU, SGU_WIDTH), 0.1),
        "sgu_ln_b": nrm(ks[13], (N_SGU, SGU_WIDTH), 0.1),
        "sgu_w_s": nrm(ks[14], (N_SGU, SGU_GROUPS, SGU_CHUNK, SGU_CHUNK), SGU_CHUNK ** -0.5),
        "sgu_b_s": 1.0 + nrm(ks[15], (N_SGU, SGU_GROUPS, SGU_CHUNK), 0.1),
        "sgu_w_out": nrm(ks[16], (N_SGU, SGU_WIDTH, D), SGU_WIDTH ** -0.5),
        "fox_w_in": nrm(ks[17], (N_FOX, D, FOX_IN), D ** -0.5),
        "fox_b_f": FORGET_BIAS_INIT + nrm(ks[18], (N_FOX, FOX_HEADS), 0.1),
        "fox_g_q": 1.0 + nrm(ks[19], (N_FOX, FOX_DH), 0.1),
        "fox_g_k": 1.0 + nrm(ks[20], (N_FOX, FOX_DH), 0.1),
        "fox_w_out": nrm(ks[21], (N_FOX, FOX_AD, D), FOX_AD ** -0.5),
    }

def first_block(x, c, norm_pre_g, norm_post_g, w_mod, b_mod,
              gla_w_in, gla_w_a2, gla_b_a, gla_g_head, gla_w_out,
              sgu_w_in, sgu_ln_g, sgu_ln_b, sgu_w_s, sgu_b_s, sgu_w_out,
              fox_w_in, fox_b_f, fox_g_q, fox_g_k, fox_w_out):
    cond = jax.nn.silu(c)
    for i in range(DEPTH):
        mod = (cond @ w_mod[i] + b_mod[i])[:, None, :]
        shift, scale, gate = jnp.split(mod, 3, axis=-1)
        h = rms_norm(x, norm_pre_g[i]) * (1.0 + scale) + shift
        kind, j = i % N_MIXERS, i // N_MIXERS
        if kind == 0:
            o = gla_mixer(h, gla_w_in[j], gla_w_a2[j], gla_b_a[j], gla_g_head[j], gla_w_out[j])
        elif kind == 1:
            o = sgu_mixer(h, sgu_w_in[j], sgu_ln_g[j], sgu_ln_b[j], sgu_w_s[j], sgu_b_s[j], sgu_w_out[j])
        else:
            o = fox_mixer(h, fox_w_in[j], fox_b_f[j], fox_g_q[j], fox_g_k[j], fox_w_out[j])
        x = x + gate * rms_norm(o, norm_post_g[i])
    return x


DEPTH_2 = 2

N_MIXERS_2 = 2
NEG_INF = -1e30

MIX_WIDTH = D_MODEL
TOK_WIDTH = 3 * MIX_WIDTH // 4
MEM_WIDTH = MIX_WIDTH // 4

DILATED_GROUPS = ((128, 1), (512, 4), (2048, 16))
ATT_HEAD_DIM = 64
ATT_HEADS = TOK_WIDTH // ATT_HEAD_DIM
HEADS_PER_GROUP = ATT_HEADS // len(DILATED_GROUPS)
BAND_BLOCK = 64
REL_BUCKETS = 32
REL_MAX_DIST = 1024

DN_HEAD_DIM = 128
DN_HEADS = TOK_WIDTH // DN_HEAD_DIM
DN_CONV = 5
DN_CHUNK = 64

MEM_LEN = 256
MEM_HEADS = 4
MEM_HEAD_DIM = MEM_WIDTH // MEM_HEADS

_FF_RAW = -(-8 * D_MODEL // 3)
D_FF = -(-_FF_RAW // 256) * 256

ATT_IN = 3 * TOK_WIDTH + MEM_WIDTH
DN_IN = 4 * TOK_WIDTH + 4 * DN_HEADS + MEM_WIDTH


def _rms_norm(x, gain):
    xf = x.astype(jnp.float32)
    y = xf * lax.rsqrt(jnp.mean(xf * xf, axis=-1, keepdims=True) + EPS) * gain.astype(jnp.float32)
    return y.astype(x.dtype)

def _l2norm(t):
    return t * lax.rsqrt(jnp.sum(t * t, axis=-1, keepdims=True) + EPS)

def _t5_bucket(rel):
    half = REL_BUCKETS // 2
    max_exact = half // 2
    n = np.abs(rel)
    large = max_exact + (np.log(np.maximum(n, 1) / max_exact) / math.log(REL_MAX_DIST / max_exact)
                         * (half - max_exact)).astype(np.int64)
    large = np.minimum(large, half - 1)
    return ((rel > 0) * half + np.where(n < max_exact, n, large)).astype(np.int32)

def _dilated_band_attention(q, k, v, bias, dil, half):
    b, s, h, dh = q.shape
    L = s // dil
    nb = -(-L // BAND_BLOCK)
    lp = nb * BAND_BLOCK
    n = b * dil

    def to_sub(t):
        return t.reshape(b, L, dil, h, dh).transpose(0, 2, 1, 3, 4).reshape(n, L, h, dh)

    def key_windows(t):
        t = jnp.pad(to_sub(t), ((0, 0), (BAND_BLOCK, lp - L + BAND_BLOCK), (0, 0), (0, 0)))
        t = t.reshape(n, nb + 2, BAND_BLOCK, h, dh)
        return jnp.concatenate([t[:, :-2], t[:, 1:-1], t[:, 2:]], axis=2)

    qs = jnp.pad(to_sub(q), ((0, 0), (0, lp - L), (0, 0), (0, 0))).reshape(n, nb, BAND_BLOCK, h, dh)
    kw = key_windows(k)
    vw = key_windows(v)

    rel = np.arange(3 * BAND_BLOCK)[None, :] - BAND_BLOCK - np.arange(BAND_BLOCK)[:, None]
    in_band = np.abs(rel) <= half
    kpos = (np.arange(nb)[:, None] - 1) * BAND_BLOCK + np.arange(3 * BAND_BLOCK)[None, :]
    valid = in_band[None] & ((kpos >= 0) & (kpos < L))[:, None, :]
    bias_band = jnp.transpose(bias[np.clip(rel + half, 0, 2 * half)], (2, 0, 1)).astype(jnp.float32)

    logits = jnp.einsum('nbqhd,nbkhd->nbhqk', qs, kw, preferred_element_type=jnp.float32)
    logits = jnp.where(valid[None, :, None], logits + bias_band[None, None], NEG_INF)
    m = jnp.max(logits, axis=-1)
    p = jnp.exp(logits - m[..., None])
    den = jnp.sum(p, axis=-1)
    o = jnp.einsum('nbhqk,nbkhd->nbqhd', p.astype(v.dtype), vw, preferred_element_type=jnp.float32)
    o = o / jnp.swapaxes(den, -1, -2)[..., None]

    def from_sub(t):
        rest = t.shape[3:]
        t = t.reshape((b, dil, lp) + rest)[:, :, :L]
        return jnp.swapaxes(t, 1, 2).reshape((b, s) + rest)

    return from_sub(o), from_sub(jnp.swapaxes(m, -1, -2)), from_sub(jnp.swapaxes(den, -1, -2))

def _dilated_mixture(q, k, v, rel_bias):
    b, s = q.shape[:2]
    outs, lses = [], []
    for gi, (window, dil) in enumerate(DILATED_GROUPS):
        half = window // (2 * dil)
        heads = slice(gi * HEADS_PER_GROUP, (gi + 1) * HEADS_PER_GROUP)
        bias = rel_bias[_t5_bucket(np.arange(-half, half + 1) * dil)][:, heads]
        o, m, den = _dilated_band_attention(q[:, :, heads], k[:, :, heads], v[:, :, heads], bias, dil, half)
        outs.append(o)
        lses.append(m + jnp.log(den))
    wts = jax.nn.softmax(jnp.stack(lses), axis=0)
    mixed = jnp.concatenate([o * w[..., None] for o, w in zip(outs, wts)], axis=2)
    return mixed.reshape(b, s, TOK_WIDTH)

def _memory_attention(q_mem, mem_n, w_kv):
    b, s, _ = q_mem.shape
    q = q_mem.reshape(b, s, MEM_HEADS, MEM_HEAD_DIM) * (MEM_HEAD_DIM ** -0.5)
    k, v = jnp.split(mem_n @ w_kv, 2, axis=-1)
    k = k.reshape(b, -1, MEM_HEADS, MEM_HEAD_DIM)
    v = v.reshape(b, -1, MEM_HEADS, MEM_HEAD_DIM)
    logits = jnp.einsum('bshd,bmhd->bhsm', q, k, preferred_element_type=jnp.float32)
    p = jax.nn.softmax(logits, axis=-1)
    o = jnp.einsum('bhsm,bmhd->bshd', p.astype(v.dtype), v)
    return o.reshape(b, s, MEM_WIDTH)

def _gated_delta_chunked(q, k, v, g, beta):
    b, s, h, dk = q.shape
    dv = v.shape[-1]
    nc = s // DN_CHUNK

    def chunks(t):
        t = t.reshape((b, nc, DN_CHUNK, h) + t.shape[3:])
        return jnp.moveaxis(t, 3, 1)

    q, k, v, g, beta = (chunks(t) for t in (q, k, v, g, beta))
    g = jnp.cumsum(g, axis=-1)
    tril = np.tril(np.ones((DN_CHUNK, DN_CHUNK), dtype=bool))
    strict = np.tril(np.ones((DN_CHUNK, DN_CHUNK), dtype=bool), -1)
    decay = jnp.exp(jnp.where(tril, g[..., :, None] - g[..., None, :], NEG_INF))
    k_beta = k * beta[..., None]
    lmat = jnp.where(strict, jnp.einsum('bhnik,bhnjk->bhnij', k_beta, k) * decay, 0.0)
    a = lmat + jnp.eye(DN_CHUNK, dtype=jnp.float32)
    rhs = jnp.concatenate([v * beta[..., None], k_beta * jnp.exp(g)[..., None]], axis=-1)
    sol = lax.linalg.triangular_solve(a, rhs, left_side=True, lower=True, unit_diagonal=True)
    u, w = sol[..., :dv], sol[..., dv:]
    intra = jnp.where(tril, jnp.einsum('bhnik,bhnjk->bhnij', q, k) * decay, 0.0)

    def step(state, inp):
        qc, kc, uc, wc, gc, ac = inp
        v_new = uc - jnp.einsum('bhck,bhkv->bhcv', wc, state)
        out = (jnp.einsum('bhck,bhkv->bhcv', qc * jnp.exp(gc)[..., None], state)
               + jnp.einsum('bhij,bhjv->bhiv', ac, v_new))
        g_last = gc[..., -1]
        state = (state * jnp.exp(g_last)[..., None, None]
                 + jnp.einsum('bhck,bhcv->bhkv', kc * jnp.exp(g_last[..., None] - gc)[..., None], v_new))
        return state, out

    xs = tuple(jnp.moveaxis(t, 2, 0) for t in (q, k, u, w, g, intra))
    state0 = jnp.zeros((b, h, dk, dv), jnp.float32)
    _, out = lax.scan(step, state0, xs)
    out = jnp.moveaxis(out, 0, 2)
    return jnp.moveaxis(out, 1, 3).reshape(b, s, h, dv)

def _attention_sublayer(h, mem_n, w_in, w_out, rel_bias, w_mem_kv):
    b, s, _ = h.shape
    q, k, v, q_mem = jnp.split(h @ w_in, [TOK_WIDTH, 2 * TOK_WIDTH, 3 * TOK_WIDTH], axis=-1)
    q = q.reshape(b, s, ATT_HEADS, ATT_HEAD_DIM) * (ATT_HEAD_DIM ** -0.5)
    k = k.reshape(b, s, ATT_HEADS, ATT_HEAD_DIM)
    v = v.reshape(b, s, ATT_HEADS, ATT_HEAD_DIM)
    mixed = _dilated_mixture(q, k, v, rel_bias).astype(h.dtype)
    mem_out = _memory_attention(q_mem, mem_n, w_mem_kv)
    return jnp.concatenate([mixed, mem_out], axis=-1) @ w_out

def _deltanet_sublayer(h, mem_n, w_in, conv_w, a_log, dt_bias, out_norm, w_out, w_mem_kv):
    b, s, _ = h.shape
    qkv, z, gate_in, q_mem = jnp.split(
        h @ w_in, [3 * TOK_WIDTH, 4 * TOK_WIDTH, 4 * TOK_WIDTH + 4 * DN_HEADS], axis=-1)
    qkv = lax.conv_general_dilated(
        qkv, conv_w[:, None, :], window_strides=(1,), padding=[(DN_CONV // 2, DN_CONV // 2)],
        dimension_numbers=('NWC', 'WIO', 'NWC'), feature_group_count=3 * TOK_WIDTH)
    q, k, v = jnp.split(jax.nn.silu(qkv).astype(jnp.float32), 3, axis=-1)
    q = _l2norm(q.reshape(b, s, DN_HEADS, DN_HEAD_DIM)) * (DN_HEAD_DIM ** -0.5)
    k = _l2norm(k.reshape(b, s, DN_HEADS, DN_HEAD_DIM))
    v = v.reshape(b, s, DN_HEADS, DN_HEAD_DIM)
    gate_in = gate_in.astype(jnp.float32).reshape(b, s, 2, 2, DN_HEADS)
    g = -jnp.exp(a_log.astype(jnp.float32)) * jax.nn.softplus(gate_in[:, :, :, 0] + dt_bias.astype(jnp.float32))
    beta = jax.nn.sigmoid(gate_in[:, :, :, 1])
    o_fwd = _gated_delta_chunked(q, k, v, g[:, :, 0], beta[:, :, 0])
    rev = lambda t: jnp.flip(t, axis=1)
    o_bwd = rev(_gated_delta_chunked(rev(q), rev(k), rev(v), rev(g[:, :, 1]), rev(beta[:, :, 1])))
    o = o_fwd + o_bwd
    zf = z.astype(jnp.float32).reshape(b, s, DN_HEADS, DN_HEAD_DIM)
    o = (o * lax.rsqrt(jnp.mean(o * o, axis=-1, keepdims=True) + EPS)
         * out_norm.astype(jnp.float32) * jax.nn.silu(zf))
    o = o.reshape(b, s, TOK_WIDTH).astype(h.dtype)
    mem_out = _memory_attention(q_mem, mem_n, w_mem_kv)
    return jnp.concatenate([o, mem_out], axis=-1) @ w_out

def _swiglu(h, w_gate_up, w_down):
    gate, up = jnp.split(h @ w_gate_up, 2, axis=-1)
    return (jax.nn.silu(gate) * up) @ w_down

def second_inputs(seed: int = 0) -> dict:
    key = jax.random.key(seed)
    ks = jax.random.split(key, 24)
    n_att = (DEPTH_2 + N_MIXERS_2 - 1) // N_MIXERS_2
    n_dn = DEPTH_2 // N_MIXERS_2

    def nrm(k, shape, scale):
        return jax.random.normal(k, shape, jnp.float32) * scale

    def gain(k, shape):
        return 1.0 + nrm(k, shape, 0.05)

    dt = jnp.exp(jax.random.uniform(ks[8], (n_dn, 2, DN_HEADS), jnp.float32,
                                    minval=math.log(1e-3), maxval=math.log(1e-1)))
    return {
        "x": nrm(ks[0], (BATCH, SEQ, D_MODEL), 1.0),
        "mem": nrm(ks[1], (BATCH, MEM_LEN, D_MODEL), 1.0),
        "rel_bias": nrm(ks[2], (REL_BUCKETS, ATT_HEADS), 0.5),
        "att_w_in": nrm(ks[3], (n_att, D_MODEL, ATT_IN), D_MODEL ** -0.5),
        "att_w_out": nrm(ks[4], (n_att, MIX_WIDTH, D_MODEL), MIX_WIDTH ** -0.5),
        "dn_w_in": nrm(ks[5], (n_dn, D_MODEL, DN_IN), D_MODEL ** -0.5),
        "dn_conv": nrm(ks[6], (n_dn, DN_CONV, 3 * TOK_WIDTH), DN_CONV ** -0.5),
        "dn_a_log": jnp.log(jax.random.uniform(ks[7], (n_dn, 2, DN_HEADS), jnp.float32, minval=1.0, maxval=16.0)),
        "dn_dt_bias": dt + jnp.log(-jnp.expm1(-dt)),
        "dn_out_norm": gain(ks[9], (n_dn, DN_HEAD_DIM)),
        "dn_w_out": nrm(ks[10], (n_dn, MIX_WIDTH, D_MODEL), MIX_WIDTH ** -0.5),
        "mem_norm": gain(ks[11], (DEPTH_2, D_MODEL)),
        "mem_w_kv": nrm(ks[12], (DEPTH_2, D_MODEL, 2 * MEM_WIDTH), D_MODEL ** -0.5),
        "norm_mix_pre": gain(ks[13], (DEPTH_2, D_MODEL)),
        "norm_mix_post": gain(ks[14], (DEPTH_2, D_MODEL)),
        "norm_ffn_pre": gain(ks[15], (DEPTH_2, D_MODEL)),
        "norm_ffn_post": gain(ks[16], (DEPTH_2, D_MODEL)),
        "ffn_w_gate_up": nrm(ks[17], (DEPTH_2, D_MODEL, 2 * D_FF), D_MODEL ** -0.5),
        "ffn_w_down": nrm(ks[18], (DEPTH_2, D_FF, D_MODEL), D_FF ** -0.5),
    }

def second_block(x, mem, rel_bias, att_w_in, att_w_out, dn_w_in, dn_conv, dn_a_log, dn_dt_bias,
              dn_out_norm, dn_w_out, mem_norm, mem_w_kv, norm_mix_pre, norm_mix_post,
              norm_ffn_pre, norm_ffn_post, ffn_w_gate_up, ffn_w_down):
    for i in range(DEPTH_2):
        j = i // N_MIXERS_2
        h = _rms_norm(x, norm_mix_pre[i])
        mem_n = _rms_norm(mem, mem_norm[i])
        if i % N_MIXERS_2 == 0:
            mixed = _attention_sublayer(h, mem_n, att_w_in[j], att_w_out[j], rel_bias, mem_w_kv[i])
        else:
            mixed = _deltanet_sublayer(h, mem_n, dn_w_in[j], dn_conv[j], dn_a_log[j], dn_dt_bias[j],
                                       dn_out_norm[j], dn_w_out[j], mem_w_kv[i])
        x = x + _rms_norm(mixed, norm_mix_post[i])
        h = _rms_norm(x, norm_ffn_pre[i])
        x = x + _rms_norm(_swiglu(h, ffn_w_gate_up[i], ffn_w_down[i]), norm_ffn_post[i])
    return x


def setup_inputs(seed=0):
    out = dict(first_inputs(seed))
    for name, value in second_inputs(seed + 1).items():
        if name != "x":
            out[name + "_2"] = value
    return out


def reference(
    x, c, norm_pre_g, norm_post_g, w_mod, b_mod, gla_w_in, gla_w_a2, gla_b_a, gla_g_head,
    gla_w_out, sgu_w_in, sgu_ln_g, sgu_ln_b, sgu_w_s, sgu_b_s, sgu_w_out, fox_w_in, fox_b_f,
    fox_g_q, fox_g_k, fox_w_out, mem_2, rel_bias_2, att_w_in_2, att_w_out_2, dn_w_in_2,
    dn_conv_2, dn_a_log_2, dn_dt_bias_2, dn_out_norm_2, dn_w_out_2, mem_norm_2, mem_w_kv_2,
    norm_mix_pre_2, norm_mix_post_2, norm_ffn_pre_2, norm_ffn_post_2, ffn_w_gate_up_2,
    ffn_w_down_2,
):
    x = first_block(
        x, c, norm_pre_g, norm_post_g, w_mod, b_mod, gla_w_in, gla_w_a2, gla_b_a, gla_g_head,
        gla_w_out, sgu_w_in, sgu_ln_g, sgu_ln_b, sgu_w_s, sgu_b_s, sgu_w_out, fox_w_in, fox_b_f,
        fox_g_q, fox_g_k, fox_w_out,
    )
    return second_block(
        x, mem_2, rel_bias_2, att_w_in_2, att_w_out_2, dn_w_in_2, dn_conv_2, dn_a_log_2,
        dn_dt_bias_2, dn_out_norm_2, dn_w_out_2, mem_norm_2, mem_w_kv_2, norm_mix_pre_2,
        norm_mix_post_2, norm_ffn_pre_2, norm_ffn_post_2, ffn_w_gate_up_2, ffn_w_down_2,
    )


_drawn_inputs = setup_inputs


def setup_inputs(seed=0):
    import zlib

    import numpy as np

    out = dict(_drawn_inputs(seed))
    spreads = {}
    factors = {'fox_b_f': 75.176, 'dn_out_norm_2': 19.72, 'fox_g_q': 3.718, 'fox_g_k': 3.915}
    for name, (base, spread) in spreads.items():
        noise = np.random.default_rng([zlib.crc32(name.encode()), seed]).standard_normal(out[name].shape)
        drawn = base * np.exp(spread * noise) if base else spread * noise
        out[name] = jnp.asarray(drawn.astype(out[name].dtype))
    for name, factor in factors.items():
        out[name] = (out[name] * factor).astype(out[name].dtype)
    return out
```

```python
from contextlib import ExitStack

import concourse.bass as bass
from concourse import mybir

F32 = mybir.dt.float32
F32R = mybir.dt.float32r
I8 = mybir.dt.int8
ALU = mybir.AluOpType
ACT = mybir.ActivationFunctionType
AX = mybir.AxisListType.X

P = 128
S = 512
TT = S // P
D = 1024
KT = D // P
BW = 512
CK = 4
EPS = 1e-6
NEG = -1e30
DEPTH = 4

GH, GDK, GDV = 4, 128, 256
GRANK = 16
LEVELS = [1, 2, 4, 8, 16, 32, 64]
SG, SGD = 4, 256
FH, FD = 16, 64
AH, AHG = 12, 4
DILS = (1, 4, 16)
HALF = 64
NBUCKET, MAXDIST = 32, 1024
MH, MD, ML = 4, 64, 256
NH = 6
CONV = 5
FF = 2816
FT = FF // P


class Group(dict):

    def __getattr__(self, name):
        return self[name]

    def __setattr__(self, name, value):
        self[name] = value


def program(nc, io, out):
    ctx = ExitStack()
    with ctx:
        def sb(name, shape, dt=F32):
            return ctx.enter_context(nc.sbuf_tensor(name, shape, dt))

        def sem(name):
            return ctx.enter_context(nc.semaphore(name))

        def sig(prefix, names):
            return Group(**{n: sem(f"{prefix}_{n}") for n in names.split()})

        PS = ctx.enter_context(nc.psum_tensor("PS", [P, 8, 512], F32))
        x = sb("x", [P, TT, D])
        with nc.sbuf_tensor("hT_a", [P, KT, S], F32) as hT_a, nc.sbuf_tensor("hT_b", [P, KT, S], F32) as hT_b:
            pass
        hT_hi = sb("hT_hi", [P, KT, S], F32R)
        hT_lo = sb("hT_lo", [P, KT, S], F32R)
        w_raw = sb("w_raw", [P, 2, CK, BW])
        w_hi = sb("w_hi", [P, 2, CK, BW], F32R)
        w_lo = sb("w_lo", [P, 2, CK, BW], F32R)
        small_raw = sb("small_raw", [P, KT, 24])
        small_hi = sb("small_hi", [P, KT, 24], F32R)
        small_lo = sb("small_lo", [P, KT, 24], F32R)
        ident = sb("ident", [P, P])
        ones = sb("ones", [P, P])
        vrows = sb("vrows", [P, P])
        vcols = sb("vcols", [P, P])
        eps = sb("eps", [P, 1])
        identr = sb("identr", [32, 32], F32R)
        cond = sb("cond", [P, KT])
        stat = sb("stat", [P, 64])
        tmp = sb("tmp", [P, D])
        ajunk = sb("ajunk", [P, BW])
        hf = tmp[:].rearrange("p (a s) -> p a s", a=2)
        modc = sb("modc", [P, 2, 2, KT])
        lvl = sb("lvl", [P, 14, P], I8)

        w_landed = [sem("w_landed0"), sem("w_landed1")]
        w_hidone = sem("w_hidone")
        w_lodone = sem("w_lodone")
        w_used = sem("w_used")
        ps_evac = sem("ps_evac")
        x_done = sem("x_done")
        out_done = sem("out_done")
        dve_own = sem("dve_own")
        act_own = sem("act_own")
        pool_own = sem("pool_own")

        own = {"dve": 0, "act": 0, "pool": 0}

        def then_dve(ins):
            own["dve"] += 1
            ins.then_inc(dve_own, 1)
            nc.vector.wait_ge(dve_own, own["dve"])

        def then_act(ins):
            own["act"] += 1
            ins.then_inc(act_own, 1)
            nc.scalar.wait_ge(act_own, own["act"])

        def then_pool(ins):
            own["pool"] += 1
            ins.then_inc(pool_own, 1)
            nc.gpsimd.wait_ge(pool_own, own["pool"])

        chunks = []
        blocks = []

        sides = Group(n=0, last=[None, None])

        def add_block(w, pieces, out=False):
            kt = w.shape[0] // P
            first = len(chunks)
            wk = w.rearrange("(k p) n -> p k n", p=P)
            sizes = []
            for k0 in range(0, kt, CK):
                k1 = min(k0 + CK, kt)
                chunks.append(([(at, n, wk[:, k0:k1, c0:c0 + n]) for at, c0, n in pieces], k1 - k0))
                sizes.append((k0, k1 - k0))
            blocks.append(Group(first=first, n=len(sizes), last=first + len(sizes) - 1, ks=sizes,
                                          index=len(blocks), out=out, half=sides.n % 2, before=sides.last[sides.n % 2],
                                          ev=sum(not b.out for b in blocks) + (not out)))
            sides.last[sides.n % 2] = blocks[-1]
            sides.n += 1
            return blocks[-1]

        def project(w, starts, out=False):
            return [add_block(w, [(0, c, BW)], out) for c in starts]

        def bank_set(b):
            return 4 * b.half

        def sp_chunk(n):
            if n >= 2:
                nc.sync.wait_ge(w_lodone, n - 1)
            for at, m, src in chunks[n][0]:
                nc.sync.dma_start(w_raw[:, n % 2, 0:chunks[n][1], at:at + m], src).then_inc(w_landed[n % 2], 16)

        landed_at = []

        def landings():
            total = [0, 0]
            for n, (pieces, _) in enumerate(chunks):
                total[n % 2] += 16 * len(pieces)
                landed_at.append(total[n % 2])

        def act_chunk(n):
            if n >= len(chunks):
                return
            k = chunks[n][1]
            m = max(at + w for at, w, _ in chunks[n][0])
            nc.scalar.wait_ge(w_landed[n % 2], landed_at[n])
            if n >= 2:
                nc.scalar.wait_ge(w_used, n - 1)
            nc.scalar.activation(w_hi[:, n % 2, 0:k, 0:m], w_raw[:, n % 2, 0:k, 0:m], ACT.Copy).then_inc(w_hidone, 1)

        def dve_chunk(n):
            if n >= len(chunks):
                return
            k = chunks[n][1]
            m = max(at + w for at, w, _ in chunks[n][0])
            nc.vector.wait_ge(w_hidone, n + 1)
            nc.vector.tensor_tensor(w_lo[:, n % 2, 0:k, 0:m], w_raw[:, n % 2, 0:k, 0:m],
                                    w_hi[:, n % 2, 0:k, 0:m].bitcast(F32), ALU.subtract).then_inc(w_lodone, 1)

        def split_ahead(split, b, full=1):
            for n in range(b.first + 2, b.last + 2 + full):
                split(n)

        def triple(o, l_hi, l_lo, r_hi, r_lo, start, stop):
            nc.tensor.matmul(o, l_hi, r_hi, start=start, stop=False)
            nc.tensor.matmul(o, l_hi, r_lo, start=False, stop=False)
            return nc.tensor.matmul(o, l_lo, r_hi, start=False, stop=stop)

        def pe_block(b, forms, a_hi, a_lo, act_ready=None):
            if b.before and not b.before.out:
                nc.tensor.wait_ge(ps_evac, b.before.ev)
            for c, (k0, kn) in enumerate(b.ks):
                n = b.first + c
                nc.tensor.wait_ge(w_lodone, n + 1)
                if act_ready and c in act_ready:
                    nc.tensor.wait_ge(*act_ready[c])
                for form in forms:
                    for k in range(kn):
                        start, stop = c == 0 and k == 0, c == b.n - 1 and k == kn - 1
                        if form[0] == "T":
                            _, bank, at = form
                            w = slice(at, at + P)
                            mm = triple(PS[:, bank, 0:a_hi.shape[2]], w_hi[:, n % 2, k, w], w_lo[:, n % 2, k, w],
                                        a_hi[:, k0 + k, :], a_lo[:, k0 + k, :], start, stop)
                        else:
                            _, bank, order, t, at, m = form
                            w = slice(at, at + m)
                            mm = triple(PS[:, bank, 0:m], order(a_hi[:, k0 + k, :], t), order(a_lo[:, k0 + k, :], t),
                                        w_hi[:, n % 2, k, w], w_lo[:, n % 2, k, w], start, stop)
                mm.then_inc(w_used, 1)

        def T_forms(b):
            return [("T", bank_set(b) + j, j * P) for j in range(4)]

        def natural_tile(a, t):
            return a[:, t * P:(t + 1) * P]

        def tok_forms(b, m=BW, at=0):
            return [("tok", bank_set(b) + t, natural_tile, t, at, m) for t in range(TT)]

        small = sig("small", "landed split mm read turned")

        def small_load(n, src, m):
            if n:
                nc.sync.wait_ge(small.split, n)
            nc.sync.dma_start(small_raw[:, :, 0:m], src).then_inc(small.landed, 16)

        def small_dve(n, m):
            nc.vector.wait_ge(small.landed, 16 * (n + 1))
            if n:
                nc.vector.wait_ge(small.mm, n)
            then_dve(nc.vector.tensor_copy(small_hi[:, :, 0:m], small_raw[:, :, 0:m]))
            nc.vector.tensor_tensor(small_lo[:, :, 0:m], small_raw[:, :, 0:m],
                                    small_hi[:, :, 0:m].bitcast(F32), ALU.subtract).then_inc(small.split, 1)

        def small_project(n, m):
            nc.tensor.wait_ge(small.split, n + 1)
            for k in range(KT):
                mm = triple(PS[0:m, 1, :], small_hi[:, k, 0:m], small_lo[:, k, 0:m], hT_hi[:, k, :], hT_lo[:, k, :],
                            k == 0, k == KT - 1)
            mm.then_inc(small.mm, 1)

        vec = {}
        vec_src = []

        def add_vec(name, src, n):
            vec[name] = sum(m for _, m in vec_src)
            vec_src.append((src, n))

        add_vec("c", io["c"].rearrange("a (r p) -> (a r) p", p=P), KT)
        add_vec("pre", io["norm_pre_g"].rearrange("l (r p) -> (l r) p", p=P), DEPTH * KT)
        add_vec("b_a", io["gla_b_a"].rearrange("l (r p) -> (l r) p", p=P), 2 * GH)
        add_vec("g_head", io["gla_g_head"].rearrange("l h (r p) -> (l h r) p", p=P), 2 * KT)
        add_vec("mix_pre", io["norm_mix_pre_2"].rearrange("l (r p) -> (l r) p", p=P), 2 * KT)
        add_vec("ffn_pre", io["norm_ffn_pre_2"].rearrange("l (r p) -> (l r) p", p=P), 2 * KT)
        add_vec("mem_norm", io["mem_norm_2"].rearrange("l (r p) -> (l r) p", p=P), 2 * KT)
        add_vec("out_norm", io["dn_out_norm_2"], 1)
        NVEC = sum(m for _, m in vec_src)

        def vcol(name, at=0, n=KT):
            return vcols[:, vec[name] + at:vec[name] + at + n]

        vec_landed = sem("vec_landed")
        x_landed = sem("x_landed")
        consts = sem("consts")
        vecT_done = sem("vecT_done")
        vcols_done = sem("vcols_done")
        cond_done = sem("cond_done")

        def sp_setup():
            at = 0
            for src, n in vec_src:
                nc.sync.dma_start(vrows[at:at + n, :], src).then_inc(vec_landed, 16)
                at += n
            nc.sync.dma_start(conv_rows, io["dn_conv_2"].rearrange("a c (r p) -> (a c r) p", p=P)).then_inc(vec_landed, 16)
            nc.sync.dma_start(x[:], io["x"].rearrange("a (t p) d -> p (a t) d", p=P)).then_inc(x_landed, 16)

            mod_loads(nc.sync, 0)

        def pool_setup():
            pool = nc.gpsimd
            pool.memset(ones[:], 1.0).then_inc(consts, 1)
            then_pool(pool.memset(ident[:], 0.0))
            pool.affine_select(out=ident[:], in_=ident[:], compare_op=ALU.not_equal, fill=1.0, base=0,
                               pattern=[[-1, P]], channel_multiplier=1).then_inc(consts, 1)
            then_pool(pool.memset(lvl[:], 0.0))
            for l, s in enumerate(LEVELS):
                nb = P // (2 * s)
                a = lvl[:, l, :].rearrange("p (b h s) -> p b h s", h=2, s=s)[:, :, 1, :]
                c = lvl[:, 7 + l, :].rearrange("p (b h s) -> p b h s", h=2, s=s)[:, :, 0, :]
                for v, lo, hi in ((a, 0, s - 1), (c, s, 2 * s - 1)):
                    then_pool(pool.memset(v, 1.0))
                    then_pool(pool.affine_select(out=v, in_=v, compare_op=ALU.is_ge, fill=0.0, base=-lo,
                                                 pattern=[[-2 * s, nb], [0, s]], channel_multiplier=1))
                    last = pool.affine_select(out=v, in_=v, compare_op=ALU.is_ge, fill=0.0, base=hi,
                                              pattern=[[2 * s, nb], [0, s]], channel_multiplier=-1)
                    if (l, lo) != (len(LEVELS) - 1, s):
                        then_pool(last)
            last.then_inc(consts, 1)

        def pe_setup():
            nc.tensor.wait_ge(consts, 2)
            nc.tensor.wait_ge(vec_landed, 16 * (len(vec_src) + 1))
            nc.tensor.transpose(PS[:, 7, P:P + CONV * 3 * NH], conv_rows, ident[0:CONV * 3 * NH, 0:CONV * 3 * NH])
            nc.tensor.transpose(PS[:, 7, 0:NVEC], vrows[0:NVEC, :], ident[0:NVEC, 0:NVEC]).then_inc(vecT_done, 1)

        def dve_setup():
            nc.vector.memset(eps[:], EPS)
            nc.vector.wait_ge(vecT_done, 1)
            nc.vector.tensor_copy(conv_cols, PS[:, 7, P:P + CONV * 3 * NH])
            nc.vector.tensor_copy(identr[:], ident[0:32, 0:32])
            nc.vector.tensor_copy(vcols[:, 0:NVEC], PS[:, 7, 0:NVEC]).then_inc(vcols_done, 1)

        conv_rows = ajunk[0:CONV * 3 * NH, 0:P]
        conv_cols = vrows[:, 0:CONV * 3 * NH]

        def act_setup():
            nc.scalar.wait_ge(vcols_done, 1)
            nc.scalar.activation(cond[:], vcol("c"), ACT.Silu).then_inc(cond_done, 1)

        MB = 3 * D // BW
        MK = 1
        m_landed = [sem(f"m_landed{s}") for s in range(4)]
        p_landed = [sem(f"p_landed{s}") for s in range(4)]
        m_used = sem("m_used")
        m_row = sem("m_row")
        mfin = sem("mfin")
        modc_done = sem("modc_done")
        G_done = sem("G_done")
        macc_zero = sem("macc_zero")
        NMC = MB * KT // MK

        first = ExitStack()
        mraw = first.enter_context(nc.sbuf_tensor("mraw", [P, 4, MK, BW], F32))
        macc = first.enter_context(nc.sbuf_tensor("macc", [P, 3 * D], F32))
        G = first.enter_context(nc.sbuf_tensor("G", [P, 2, D], F32))

        MS = 4

        def mod_loads(eng, i):
            w = io["w_mod"][i].rearrange("(k p) n -> p k n", p=P)
            for m in range(MB):
                for c in range(KT // MK):
                    n = i * NMC + m * (KT // MK) + c
                    if n >= MS:
                        eng.wait_ge(m_used, n - MS + 1)
                    eng.dma_start(mraw[:, n % MS], w[:, c * MK:(c + 1) * MK, m * BW:(m + 1) * BW]) \
                        .then_inc((p_landed if i else m_landed)[n % MS], 16)

        def pool_mod(i):
            pool = nc.gpsimd
            if i >= 1:
                pool.wait_ge(mfin, i)
            pool.memset(macc[:], 0.0).then_inc(macc_zero, 1)
            pool.wait_ge(macc_zero, i + 1)
            pool.dma_start(macc[0:1, :], io["b_mod"][i:i + 1, :]).then_inc(m_row, 16)
            if i >= 2:
                pool.wait_ge(x_done, TT * (i - 1))
            pool.dma_start(G[:, i % 2, :], bass.AP(io["norm_post_g"].tensor, i * D, [[0, P], [1, D]])).then_inc(m_row, 16)
            if i:
                mod_loads(pool, i)

        def dve_mod(i, m):
            if m == 0:
                nc.vector.wait_ge(m_row, 32 * (i + 1))
            if i == 0 and m == 0:
                nc.vector.wait_ge(cond_done, 1)
            acc = macc[:, m * BW:(m + 1) * BW]
            for c in range(KT // MK):
                n = i * NMC + m * (KT // MK) + c
                if i == 0:
                    nc.vector.wait_ge(m_landed[n % MS], 16 * (n // MS + 1))
                else:
                    nc.vector.wait_ge(p_landed[n % MS], 16 * ((n - NMC) // MS + 1))
                for k in range(MK):
                    ins = nc.vector.scalar_tensor_tensor(out=acc, in0=mraw[:, n % MS, k, :],
                                                         scalar=cond[:, c * MK + k:c * MK + k + 1], in1=acc,
                                                         op0=ALU.mult, op1=ALU.add)
                    if k < MK - 1:
                        then_dve(ins)
                    else:
                        ins.then_inc(m_used, 1)
                        nc.vector.wait_ge(m_used, n + 1)

        def pe_mod(i, banks):
            nc.tensor.wait_ge(m_used, NMC * (i + 1))
            for j in range(2 * KT):
                nc.tensor.matmul(PS[:, banks[0], 2 * j:2 * j + 1], macc[:, j * P:(j + 1) * P], ones[:, 0:1],
                                 start=True, stop=True)
            for j in range(2):
                mm = nc.tensor.matmul(PS[:, banks[1 + j], :], ones[:], macc[:, (4 + j) * BW:(5 + j) * BW],
                                      start=True, stop=True)
            mm.then_inc(mfin, 1)

        def dve_modfin(i, banks):
            v = PS[:, banks[0], 0:4 * KT].rearrange("p (j e) -> p j e", e=2)[:, :, 0]
            nc.vector.wait_ge(mfin, i + 1)
            nc.vector.tensor_copy(modc[:, i % 2, 1, :], v[:, 0:KT])
            nc.vector.scalar_tensor_tensor(out=modc[:, i % 2, 0, :], in0=v[:, KT:2 * KT], scalar=1.0,
                                           in1=vcol("pre", KT * i), op0=ALU.add, op1=ALU.mult).then_inc(modc_done, 1)
            for j in range(2):
                g = G[:, i % 2, j * BW:(j + 1) * BW]
                ins = nc.vector.tensor_tensor(g, g, PS[:, banks[1 + j], :], ALU.mult)
            ins.then_inc(G_done, 1)

        pre_x = sig("pre", "sq sd xnd tr hf split")

        def norm_front(q, m):
            sides.n, sides.last = 0, [None, None]
            q.late = blocks[-1].last + 2 if blocks else None
            q.pre, q.tb, q.kb = pre_x, TT * m, KT * m
            q.split_ready = {0: (pre_x.split, KT * m + CK), 1: (pre_x.split, KT * m + KT)}
            q.region_free = (pre_x.tr, TT * (m + 1))

        def pre_act(q, xw, scale, bias, src=None, nt=TT, ready=None):
            src = x if src is None else src
            for t in range(nt):
                nc.scalar.wait_ge(*xw(t))
                nc.scalar.activation(q.xn[:, t, :], src[:, t, :], ACT.Square, scale=float(D) ** -0.5,
                                     accum_out=q.st[:, t:t + 1]).then_inc(q.pre.sq, 1)
                nc.scalar.wait_ge(q.pre.sq, q.tb + t + 1)
                nc.scalar.activation(q.st[:, 8 + t:9 + t], q.st[:, t:t + 1], ACT.Sqrt, bias=eps[:]).then_inc(q.pre.sd, 1)
            if q.late is not None:
                act_chunk(q.late)
            if ready:
                nc.scalar.wait_ge(*ready)
            for k in range(KT):
                if k == 0:
                    nc.scalar.wait_ge(q.pre.tr, q.tb + nt)
                if k >= 2:
                    nc.scalar.wait_ge(q.pre.split, q.kb + k - 1)
                nc.scalar.activation(hf[:, k % 2, 0:nt * P], PS[:, k, 0:nt * P], ACT.Identity, scale=scale[:, k:k + 1],
                                     bias=bias[:, k:k + 1] if bias is not None else 0.0).then_inc(q.pre.hf, 1)

        def pre_dve(q, a_hi, a_lo, src=None, nt=TT):
            src = x if src is None else src
            for t in range(nt):
                nc.vector.wait_ge(q.pre.sd, q.tb + t + 1)
                then_dve(nc.vector.reciprocal(q.st[:, 12 + t:13 + t], q.st[:, 8 + t:9 + t]))
                nc.vector.tensor_scalar(q.xn[:, t, :], src[:, t, :], q.st[:, 12 + t:13 + t], None, ALU.mult).then_inc(q.pre.xnd, 1)
            if q.late is not None:
                dve_chunk(q.late)
            for k in range(KT):
                nc.vector.wait_ge(q.pre.hf, q.kb + k + 1)
                then_dve(nc.vector.tensor_copy(a_hi[:, k, :], hf[:, k % 2, 0:nt * P]))
                nc.vector.tensor_tensor(a_lo[:, k, :], hf[:, k % 2, 0:nt * P], a_hi[:, k, :].bitcast(F32),
                                        ALU.subtract).then_inc(q.pre.split, 1)

        def pre_pe(q, banks_free, nt=TT):
            for w in banks_free:
                nc.tensor.wait_ge(*w)
            for t in range(nt):
                nc.tensor.wait_ge(q.pre.xnd, q.tb + t + 1)
                for k in range(KT):
                    mm = nc.tensor.transpose(PS[:, k, t * P:(t + 1) * P], q.xn[:, t, k * P:(k + 1) * P], ident[:])
                mm.then_inc(q.pre.tr, 1)

        post = sig("post", "psq peps psd")

        def post_act(q, bb):
            for h, b in enumerate(bb):
                split_ahead(act_chunk, b, 1 - h)
                nc.scalar.wait_ge(w_used, b.last + 1)
                for t in range(TT):
                    if h or t:
                        nc.scalar.wait_ge(post.psq, 2 * q.tb + TT * h + t)
                    nc.scalar.activation(ajunk[:, 0:BW], PS[:, bank_set(b) + t, :], ACT.Square, scale=float(D) ** -0.5,
                                         accum_out=q.st[:, 16 + 2 * t + h:17 + 2 * t + h]).then_inc(post.psq, 1)
                    if h:
                        nc.scalar.wait_ge(post.psq, 2 * q.tb + 5 + t)
                        nc.scalar.wait_ge(post.peps, q.tb + t + 1)
                        nc.scalar.activation(q.st[:, 28 + t:29 + t], q.st[:, 17 + 2 * t:18 + 2 * t], ACT.Sqrt,
                                             bias=q.st[:, 24 + t:25 + t]).then_inc(post.psd, 1)

        def post_dve(q, bb, Grow, g_ready, xd):
            split_ahead(dve_chunk, bb[0])
            split_ahead(dve_chunk, bb[1], 0)
            nc.vector.wait_ge(*g_ready)
            for t in range(TT):
                nc.vector.wait_ge(post.psq, 2 * q.tb + 1 + t)
                nc.vector.tensor_scalar(q.st[:, 24 + t:25 + t], q.st[:, 16 + 2 * t:17 + 2 * t], EPS, None,
                                        ALU.add).then_inc(post.peps, 1)
            nc.vector.wait_ge(w_used, bb[1].last + 1)
            for t in range(TT):
                nc.vector.wait_ge(post.psd, q.tb + t + 1)
                if t == 0:
                    nc.vector.wait_ge(post.psq, 2 * q.tb + 8)
                then_dve(nc.vector.reciprocal(q.st[:, 32 + t:33 + t], q.st[:, 28 + t:29 + t]))
                for h, b in enumerate(bb):
                    ins = nc.vector.scalar_tensor_tensor(out=tmp[:, h * BW:(h + 1) * BW], in0=PS[:, bank_set(b) + t, :],
                                                         scalar=q.st[:, 32 + t:33 + t], in1=Grow[:, h * BW:(h + 1) * BW],
                                                         op0=ALU.mult, op1=ALU.mult)
                then_dve(ins)
                nc.vector.tensor_tensor(x[:, t, :], x[:, t, :], tmp[:], ALU.add).then_inc(x_done, 1)

        def region(stack, **shapes):
            e = ExitStack()
            made = {n: e.enter_context(nc.sbuf_tensor(f"{stack}_{n}", v[0], v[1] if len(v) > 1 else F32))
                    for n, v in shapes.items()}
            e.close()
            return Group(**made)

        gla_s = sig("gla", "lowTd wa2 lg lab b_done e ex kq pe_e dg cp kxs kv s o osq rstd on ot os at0 dec qx")

        def gla_layer(i, j, xw):
            q = Group(gla_s)
            norm_front(q, i)
            q.st = stat
            r = region(f"gla{j}", qT=([P, GH, S],), kT=([P, GH, S],), v=([P, TT, D],), szT=([P, KT, S],),
                       lowT=([GRANK, S],), wa2=([GRANK, GH * GDK],), E=([P, 2, S],),
                       AT=([P, TT, P],), QX=([P, S],), KXT=([P, TT, P],), St=([P, 3, GDV],), o=([P, TT, GDV],),
                       dec=([P, TT],))
            q.xn = region(f"gla{j}x", xn=([P, TT, D],)).xn
            w = io["gla_w_in"][j]
            wb = project(w, [c * BW for c in range(6)])
            ob = project(io["gla_w_out"][j], [0, BW], out=True)
            NE = 8
            g_small = w.rearrange("(k p) n -> p k n", p=P)[:, :, 6 * BW:6 * BW + GRANK]

            heads = [(h, GH * j + h) for h in range(GH)]
            b_ = lambda h: hT_b[:, GH + h, :]
            z_ = hT_a[:, GH:2 * GH, :]
            LB = (7, 4, 5, 6)

            def load():
                small_load(2 * j, g_small, GRANK)
                for n in range(wb[0].first, wb[-1].last + 1):
                    sp_chunk(n)
                nc.sync.dma_start(r.wa2[:], io["gla_w_a2"][j]).then_inc(q.wa2, 16)
                for n in range(ob[0].first, ob[-1].last + 1):
                    sp_chunk(n)

            def pe():
                pe_ = nc.tensor
                pre_pe(q, [])
                for n, b in enumerate(wb):
                    pe_block(b, tok_forms(b) if n in (2, 3) else T_forms(b), hT_hi, hT_lo,
                             q.split_ready if n == 0 else None)
                pe_.wait_ge(ps_evac, wb[-1].ev)
                small_project(2 * j, GRANK)
                pe_.wait_ge(q.wa2, 16 * (j + 1))
                pe_.wait_ge(q.lowTd, j + 1)
                for h, g in heads:
                    pe_.matmul(PS[:, LB[h], :], r.wa2[:, h * GDK:(h + 1) * GDK], r.lowT[:], start=True, stop=True).then_inc(q.lg, 1)

                def turn(g):
                    pe_.wait_ge(q.on, g + 1)
                    if g % GH:
                        pe_.wait_ge(q.os, 2 * g)
                    for t in range(TT):
                        for f in range(2):
                            mm = pe_.transpose(PS[:, 3 + f, t * P:(t + 1) * P], r.o[:, t, f * P:(f + 1) * P], ident[:])
                    mm.then_inc(q.ot, 1)

                for h, g in heads:
                    pe_.wait_ge(q.kq, NE * g + 1)
                    if g:
                        pe_.wait_ge(q.kxs, g)
                    for t in range(TT):
                        mm = pe_.transpose(PS[:, 2, t * P:(t + 1) * P], r.E[:, 0, t * P:(t + 1) * P], ident[:])
                    mm.then_inc(q.pe_e, 1)
                    for l in range(NE):
                        c = NE * g + l
                        if c >= 2:
                            pe_.wait_ge(q.cp, c - 1)
                        if l:
                            pe_.wait_ge(q.kq, c + 1)
                        for t in range(TT):
                            ts = slice(t * P, (t + 1) * P)
                            a, m = (r.kT[:, h, ts], r.qT[:, h, ts]) if l == 0 else (r.E[:, c % 2, ts], r.E[:, c % 2, ts])
                            mm = pe_.matmul(PS[:, l % 2, ts], a, m, start=True, stop=True)
                        mm.then_inc(q.pe_e if l else q.dg, 1)
                        if l == 5 and h:
                            turn(g - 1)
                    if h == 0:
                        pe_.wait_ge(q.b_done, GH * (j + 1))
                    if g:
                        pe_.wait_ge(q.os, 2 * g)
                    pe_.wait_ge(q.kxs, g + 1)
                    for t in range(3):
                        mm = pe_.matmul(PS[:, 3 + t // 2, (t % 2) * GDV:(t % 2 + 1) * GDV], r.KXT[:, t, :],
                                        r.v[:, t, h * GDV:(h + 1) * GDV], start=True, stop=True)
                    mm.then_inc(q.kv, 1)
                    if g:
                        pe_.wait_ge(q.on, g)
                    pe_.wait_ge(q.cp, NE * (g + 1))
                    pe_.wait_ge(q.qx, g + 1)
                    for t in range(TT):
                        o = PS[:, 5 + t // 2, (t % 2) * GDV:(t % 2 + 1) * GDV]
                        mm = pe_.matmul(o, r.AT[:, t, :], r.v[:, t, h * GDV:(h + 1) * GDV], start=True, stop=t == 0)
                        if t:
                            pe_.wait_ge(q.s, 3 * g + t)
                            mm = pe_.matmul(o, r.QX[:, t * P:(t + 1) * P], r.St[:, t - 1, :], start=False, stop=True)
                    mm.then_inc(q.o, 1)
                if i + 1 < DEPTH:
                    pe_mod(i + 1, (2, 0, 1))
                turn(heads[-1][1])
                if i + 1 < DEPTH:
                    pe_.wait_ge(G_done, i + 2)
                pe_.wait_ge(q.os, KT * (j + 1))
                for b in ob:
                    pe_block(b, tok_forms(b), hT_hi, hT_lo)

            def act():
                a = nc.scalar
                pre_act(q, xw, modc[:, i % 2, 0, :], modc[:, i % 2, 1, :], ready=(modc_done, i + 1))
                for n, b in enumerate(wb):
                    split_ahead(act_chunk, b)
                    a.wait_ge(w_used, b.last + 1)
                    s = bank_set(b)
                    if n == 0:
                        a.activation(r.qT[:], PS[:, s:s + 4, :], ACT.Copy, scale=float(GDK) ** -0.5).then_inc(ps_evac, 1)
                    elif n == 1:
                        a.activation(r.kT[:], PS[:, s:s + 4, :], ACT.Copy).then_inc(ps_evac, 1)
                    elif n < 4:
                        a.activation(r.v[:, :, (n - 2) * BW:(n - 1) * BW], PS[:, s:s + 4, :], ACT.Copy).then_inc(ps_evac, 1)
                    else:
                        a.activation(r.szT[:, 4 * (n - 4):4 * (n - 3), :], PS[:, s:s + 4, :], ACT.Silu).then_inc(ps_evac, 1)
                for h, g in heads:
                    a.wait_ge(q.lg, g + 1)
                    ins = a.activation(z_[:, h, :], PS[:, LB[h], :], ACT.Abs, bias=vcol("b_a", GH * j + h, 1))
                then_act(ins)
                then_act(a.activation(z_, z_, ACT.Exp, scale=-1.0))
                a.activation(z_, z_, ACT.Ln, bias=1.0).then_inc(q.lab, 1)

                def squares(g):
                    a.wait_ge(q.o, g + 1)
                    for t in range(TT):
                        a.activation(ajunk[:, 0:GDV], PS[:, 5 + t // 2, (t % 2) * GDV:(t % 2 + 1) * GDV], ACT.Square,
                                     scale=float(GDV) ** -0.5, accum_out=stat[:, 40 + t:41 + t]).then_inc(q.osq, 1)
                        a.wait_ge(q.osq, TT * g + t + 1)
                    a.activation(stat[:, 44:48], stat[:, 40:44], ACT.Sqrt, bias=eps[:]).then_inc(q.rstd, 1)

                for h, g in heads:
                    for l in range(NE):
                        c = NE * g + l
                        a.wait_ge(q.e, c + 1)
                        a.activation(r.E[:, c % 2, :], r.E[:, c % 2, :], ACT.Exp, scale=1 / 16).then_inc(q.ex, 1)
                        if l == 1:
                            a.wait_ge(q.pe_e, NE * g + 1)
                            if g:
                                a.wait_ge(q.kv, g)
                            a.activation(r.KXT[:].rearrange("p t s -> p (t s)"), PS[:, 2, :], ACT.Copy).then_inc(q.kxs, 1)
                        if l == 2:
                            if g:
                                a.wait_ge(q.o, g)
                            a.activation(r.dec[:], b_(h).rearrange("p (t s) -> p t s", t=TT)[:, :, P - 1], ACT.Exp,
                                         scale=1 / 16).then_inc(q.dec, 1)
                            a.activation(r.QX[:], b_(h), ACT.Exp, scale=1 / 16).then_inc(q.dec, 1)
                        if l == 3 and h:
                            squares(g - 1)
                squares(heads[-1][1])
                post_act(q, ob)

            def pool():
                p = nc.gpsimd
                if i + 1 < DEPTH:
                    pool_mod(i + 1)
                p.wait_ge(ps_evac, wb[-1].ev)
                p.memset(r.AT[:], 0.0).then_inc(q.at0, 1)
                for h, g in heads:
                    p.wait_ge(q.b_done, g + 1)
                    bt = b_(h).rearrange("p (t s) -> p t s", t=TT)
                    for l in range(NE):
                        c = NE * g + l
                        if c >= 2:
                            p.wait_ge(q.pe_e, c - 1)
                        e = r.E[:, c % 2, :]
                        if l == 0:
                            p.tensor_tensor(e.rearrange("p (t s) -> p t s", t=TT),
                                            bt[:, :, P - 1:P].to_broadcast([P, TT, P]), bt, ALU.subtract).then_inc(q.e, 1)
                            continue
                        s = LEVELS[l - 1]
                        ev = e.rearrange("p (n z s) -> p n z s", z=2, s=s)
                        bv = b_(h).rearrange("p (n z s) -> p n z s", z=2, s=s)
                        ref = bv[:, :, 0, s - 1:s].to_broadcast([P, S // (2 * s), s])
                        p.tensor_tensor(ev[:, :, 1, :], bv[:, :, 1, :], ref, ALU.subtract)
                        p.tensor_tensor(ev[:, :, 0, :], ref, bv[:, :, 0, :], ALU.subtract).then_inc(q.e, 1)

            def dve():
                v = nc.vector
                pre_dve(q, hT_hi, hT_lo)
                small_dve(2 * j, GRANK)
                for m, b in enumerate(wb):
                    split_ahead(dve_chunk, b)
                    if i + 1 < DEPTH and m < MB - 1:
                        dve_mod(i + 1, m)
                v.wait_ge(small.mm, 2 * j + 1)
                v.tensor_copy(r.lowT[:], PS[0:GRANK, 1, :]).then_inc(q.lowTd, 1)
                if i + 1 < DEPTH:
                    dve_mod(i + 1, MB - 1)
                v.wait_ge(q.at0, j + 1)
                v.wait_ge(q.lab, j + 1)
                for h, g in heads:
                    then_dve(v.tensor_scalar(b_(h), PS[:, LB[h], :], vcol("b_a", GH * j + h, 1), 0.0, ALU.add, ALU.min))
                    then_dve(v.tensor_tensor(b_(h), b_(h), z_[:, h, :], ALU.subtract))
                    for t in range(TT):
                        ts = slice(t * P, (t + 1) * P)
                        ins = v.tensor_tensor_scan(b_(h)[:, ts], ones[:], b_(h)[:, ts], 0.0, ALU.mult, ALU.add)
                    ins.then_inc(q.b_done, 1)

                def normalise(g):
                    v.wait_ge(q.rstd, g + 1)
                    if g % GH:
                        v.wait_ge(q.ot, g)
                    then_dve(v.reciprocal(stat[:, 52:56], stat[:, 44:48]))
                    for t in range(TT):
                        ins = v.tensor_scalar(r.o[:, t, :], PS[:, 5 + t // 2, (t % 2) * GDV:(t % 2 + 1) * GDV],
                                              stat[:, 52 + t:53 + t], None, ALU.mult)
                    ins.then_inc(q.on, 1)

                def gate(h, g):
                    v.wait_ge(q.ot, g + 1)
                    for f in range(2):
                        k = 2 * h + f
                        then_dve(v.scalar_tensor_tensor(out=hf[:, f, :], in0=PS[:, 3 + f, :], scalar=vcol("g_head", KT * j + k, 1),
                                                        in1=r.szT[:, k, :], op0=ALU.mult, op1=ALU.mult))
                        then_dve(v.tensor_copy(hT_hi[:, k, :], hf[:, f, :]))
                        v.tensor_tensor(hT_lo[:, k, :], hf[:, f, :], hT_hi[:, k, :].bitcast(F32), ALU.subtract).then_inc(q.os, 1)

                for h, g in heads:

                    def copy_level(l):
                        c = NE * g + l
                        v.wait_ge(*((q.pe_e, c + 1) if l else (q.dg, g + 1)))
                        mask = ident[:].bitcast(mybir.dt.int32) if l == 0 else lvl[:, l - 1, :]
                        if l == 0 and g:
                            v.wait_ge(q.o, g)
                        if c:
                            v.wait_ge(q.cp, c)
                        v.copy_predicated(r.AT[:], mask.unsqueeze(1).to_broadcast([P, TT, P]),
                                          PS[:, l % 2, :].rearrange("p (t s) -> p t s", t=TT)).then_inc(q.cp, 1)

                    for l in range(NE):
                        c = NE * g + l
                        e = r.E[:, c % 2, :]
                        v.wait_ge(q.ex, c + 1)
                        if l == 0:
                            v.tensor_tensor(e, e, r.kT[:, h, :], ALU.mult).then_inc(q.kq, 1)
                            continue
                        s = LEVELS[l - 1]
                        ev = e.rearrange("p (n z s) -> p n z s", z=2, s=s)
                        for z, a in ((0, r.kT), (1, r.qT)):
                            ins = v.tensor_tensor(ev[:, :, z, :], ev[:, :, z, :],
                                                  a[:, h, :].rearrange("p (n z s) -> p n z s", z=2, s=s)[:, :, z, :], ALU.mult)
                        ins.then_inc(q.kq, 1)
                        copy_level(l - 1)
                        if l == 3:
                            v.wait_ge(q.dec, 2 * g + 2)
                            v.tensor_tensor(r.QX[:], r.QX[:], r.qT[:, h, :], ALU.mult).then_inc(q.qx, 1)
                        if l == 4 and h:
                            normalise(g - 1)
                        if l == 6 and h:
                            gate(h - 1, g - 1)
                    copy_level(NE - 1)
                    v.wait_ge(q.kv, g + 1)
                    for t in range(3):
                        kv = PS[:, 3 + t // 2, (t % 2) * GDV:(t % 2 + 1) * GDV]
                        if t == 0:
                            ins = v.tensor_copy(r.St[:, 0, :], kv)
                        else:
                            ins = v.scalar_tensor_tensor(out=r.St[:, t, :], in0=r.St[:, t - 1, :], scalar=r.dec[:, t:t + 1],
                                                         in1=kv, op0=ALU.mult, op1=ALU.add)
                        ins.then_inc(q.s, 1)
                        v.wait_ge(q.s, 3 * g + t + 1)
                normalise(heads[-1][1])
                if i + 1 < DEPTH:
                    dve_modfin(i + 1, (2, 0, 1))
                gate(*heads[-1])
                post_dve(q, ob, G[:, i % 2, :], (G_done, i + 1), None)

            return Group(load=load, pe=pe, act=act, pool=pool, dve=dve)

        def sgu_layer(i, j, xw):
            q = sig(f"sgu{j}", "rows ws_in ws_masked wsT wsTd bs_in st_done us mix os lsd vn")
            q.st = stat
            norm_front(q, i)
            r = region(f"sgu{j}", v=([P, TT, D],), usT=([P, KT, S],), zt=([P, TT, S],), g=([P, D],), b=([P, D],),
                       ws=([P, SG, P],), wsT=([P, SG, P],), bs=([1, SG * P],), bn=([P, TT, 2, 6],), mv=([P, TT, 2],),
                       rs=([P, TT],))
            q.xn = region(f"sgu{j}x", xn=([P, TT, D],)).xn
            wb = project(io["sgu_w_in"][j], [2 * BW, 3 * BW, 0, BW, 4 * BW, 5 * BW])
            ob = project(io["sgu_w_out"][j], [0, BW], out=True)

            def load():
                for n in range(wb[0].first, wb[-1].last + 1):
                    sp_chunk(n)
                    if n == wb[0].first + 1:
                        sp = nc.sync
                        sp.wait_ge(*q.region_free)
                        for row, name in ((r.g, "sgu_ln_g"), (r.b, "sgu_ln_b")):
                            sp.dma_start(row[:], bass.AP(io[name].tensor, j * D, [[0, P], [1, D]])).then_inc(q.rows, 16)
                        sp.dma_start(r.ws[:], io["sgu_w_s"][j].rearrange("g t s -> t g s")).then_inc(q.ws_in, 16)
                        sp.dma_start(r.bs[:], io["sgu_b_s"][j:j + 1].rearrange("a g t -> a (g t)")).then_inc(q.bs_in, 16)
                for n in range(ob[0].first, ob[-1].last + 1):
                    sp_chunk(n)

            def pe():
                t_ = nc.tensor
                pre_pe(q, [])
                for n, b in enumerate(wb):
                    pe_block(b, tok_forms(b) if n < 2 else T_forms(b), hT_hi, hT_lo,
                             q.split_ready if n == 0 else None)
                t_.wait_ge(ps_evac, wb[-1].ev)
                t_.wait_ge(q.ws_masked, 1)
                for g in range(SG):
                    mm = t_.transpose(PS[:, 0, g * P:(g + 1) * P], r.ws[:, g, :], ident[:])
                mm.then_inc(q.wsT, 1)
                if i + 1 < DEPTH:
                    pe_mod(i + 1, (3, 5, 6))
                t_.wait_ge(q.wsTd, 1)
                t_.wait_ge(q.bs_in, 16)
                t_.wait_ge(q.vn, TT)
                for k in range(KT):
                    g = k * P // SGD
                    if k == 3 and i + 1 < DEPTH:
                        t_.wait_ge(G_done, i + 2)
                    for c in range(TT):
                        o = PS[:, k, c * P:(c + 1) * P]
                        t_.matmul(o, r.v[:, c, k * P:(k + 1) * P], r.wsT[:, g, :], start=True, stop=False)
                        mm = t_.matmul(o, ones[0:1, :], r.bs[:, g * P:(g + 1) * P], start=False, stop=True)
                    mm.then_inc(q.mix, 1)
                t_.wait_ge(q.os, KT)
                for b in ob:
                    pe_block(b, tok_forms(b), hT_hi, hT_lo)

            def act():
                a = nc.scalar
                pre_act(q, xw, modc[:, i % 2, 0, :], modc[:, i % 2, 1, :], ready=(modc_done, i + 1))
                for n, b in enumerate(wb):
                    split_ahead(act_chunk, b)
                    a.wait_ge(w_used, b.last + 1)
                    s = bank_set(b)
                    if n < 2:
                        a.activation(r.v[:, :, n * BW:(n + 1) * BW], PS[:, s:s + 4, :], ACT.Gelu_apprx_tanh).then_inc(ps_evac, 1)
                    elif n < 4:
                        a.activation(r.usT[:, 4 * (n - 2):4 * (n - 1), :], PS[:, s:s + 4, :], ACT.Gelu_apprx_tanh).then_inc(ps_evac, 1)
                    else:
                        if n == 5:
                            a.wait_ge(q.us, 1)
                        a.activation(r.zt[:], PS[:, s:s + 4, :], ACT.Silu).then_inc(ps_evac, 1)
                    if n == 2:
                        a.wait_ge(q.st_done, 1)
                        a.activation(r.rs[:], r.mv[:, :, 1], ACT.Sqrt).then_inc(q.lsd, 1)
                post_act(q, ob)

            def pool():
                if i + 1 < DEPTH:
                    pool_mod(i + 1)
                nc.gpsimd.wait_ge(q.ws_in, 16)
                nc.gpsimd.affine_select(out=r.ws[:], in_=r.ws[:], compare_op=ALU.is_ge, fill=0.0, base=0,
                                        pattern=[[0, SG], [-1, P]], channel_multiplier=1).then_inc(q.ws_masked, 1)

            def dve():
                v = nc.vector
                pre_dve(q, hT_hi, hT_lo)
                for m, b in enumerate(wb):
                    split_ahead(dve_chunk, b)
                    if m == 2:
                        v.wait_ge(ps_evac, wb[1].ev)
                        for t in range(TT):
                            for h in range(2):
                                ins = v.bn_stats(r.bn[:, t, h, :], r.v[:, t, h * BW:(h + 1) * BW])
                        then_dve(ins)
                        for t in range(TT):
                            ins = v.bn_aggr(r.mv[:, t, :], r.bn[:, t].rearrange("p a c -> p (a c)"))
                        then_dve(ins)
                        v.tensor_scalar(r.mv[:, :, 1], r.mv[:, :, 1], EPS, None, ALU.add).then_inc(q.st_done, 1)
                    if i + 1 < DEPTH:
                        dve_mod(i + 1, m)
                    if m == 3:
                        v.wait_ge(q.lsd, 1)
                        v.wait_ge(q.rows, 32)
                        then_dve(v.reciprocal(r.mv[:, :, 1], r.rs[:]))
                        for t in range(TT):
                            vt = r.v[:, t, :]
                            then_dve(v.tensor_scalar(vt, vt, r.mv[:, t, 0:1], r.mv[:, t, 1:2], ALU.subtract, ALU.mult))
                            then_dve(v.tensor_tensor(vt, vt, r.g[:], ALU.mult))
                            v.tensor_tensor(vt, vt, r.b[:], ALU.add).then_inc(q.vn, 1)
                    if m >= 4:
                        v.wait_ge(ps_evac, b.ev)
                        u = r.usT[:, 4 * (m - 4):4 * (m - 3), :]
                        v.tensor_tensor(u, u, r.zt[:], ALU.mult).then_inc(q.us, 1)
                v.wait_ge(q.wsT, 1)
                v.tensor_copy(r.wsT[:].rearrange("p g t -> p (g t)"), PS[:, 0, :]).then_inc(q.wsTd, 1)
                if i + 1 < DEPTH:
                    dve_modfin(i + 1, (3, 5, 6))
                v.wait_ge(q.us, 2)
                for k in range(KT):
                    v.wait_ge(q.mix, k + 1)
                    then_dve(v.tensor_tensor(hf[:, k % 2, :], PS[:, k, :], r.usT[:, k, :], ALU.mult))
                    then_dve(v.tensor_copy(hT_hi[:, k, :], hf[:, k % 2, :]))
                    v.tensor_tensor(hT_lo[:, k, :], hf[:, k % 2, :], hT_hi[:, k, :].bitcast(F32), ALU.subtract).then_inc(q.os, 1)
                post_dve(q, ob, G[:, i % 2, :], (G_done, i + 1), None)

            return Group(load=load, pe=pe, act=act, pool=pool, dve=dve)

        lens = sig("lens", "sq sum root rows nrm")

        fox_s = sig("fox", "cols lz f1 F_done cm bones FRm FR sc ttr ex scl pt pts pv os")

        def norm_heads(base, n_tiles, per, bank, banks, sums, sq, tile, gain, rows_at, spread):
            nr = per * n_tiles
            W = P // per
            rr, rhi, rlo = (z[0:nr] for z in rows_at)

            def pe():
                t_ = nc.tensor
                for n in range(n_tiles):
                    t_.wait_ge(lens.sq, base.sq + n + 1)
                    t_.matmul(PS[0:nr, bank, :], sums[:, nr - per * n:2 * nr - per * n], sq(n), start=n == 0,
                              stop=n == n_tiles - 1).then_inc(lens.sum, 1)
                t_.wait_ge(lens.rows, base.rows + 1)
                for n in range(n_tiles):
                    if n >= 2:
                        t_.wait_ge(lens.nrm, base.nrm + n - 1)
                    t_.matmul(PS[:, banks[n % 2], :], spread(n), rhi, start=True, stop=False)
                    t_.matmul(PS[:, banks[n % 2], :], spread(n), rlo, start=False, stop=True).then_inc(lens.sum, 1)

            def act(src):
                for n in range(n_tiles):
                    if n >= 2:
                        nc.scalar.wait_ge(lens.sum, base.sum + n - 1)
                    nc.scalar.activation(sq(n), src(n), ACT.Square, scale=float(W) ** -0.5 if per == 2 else 1.0).then_inc(lens.sq, 1)
                nc.scalar.wait_ge(lens.sum, base.sum + n_tiles)
                nc.scalar.activation(rr, PS[0:nr, bank, :], ACT.Sqrt, bias=eps[0:nr]).then_inc(lens.root, 1)

            def dve():
                v = nc.vector
                v.wait_ge(lens.root, base.root + 1)
                then_dve(v.reciprocal(rr, rr))
                then_dve(v.tensor_copy(rhi, rr))
                v.tensor_tensor(rlo, rr, rhi.bitcast(F32), ALU.subtract).then_inc(lens.rows, 1)
                for n in range(n_tiles):
                    v.wait_ge(lens.sum, base.sum + n_tiles + n + 1)
                    v.scalar_tensor_tensor(out=tile(n), in0=tile(n), scalar=gain(n), in1=PS[:, banks[n % 2], :],
                                           op0=ALU.mult, op1=ALU.mult).then_inc(lens.nrm, 1)

            return Group(pe=pe, act=act, dve=dve)

        def fox_layer(i, j, xw):
            q = Group(fox_s)
            q.nrm = lens.nrm
            q.st = stat
            norm_front(q, i)
            NP = FH // 2
            r = region(f"fox{j}", qT=([P, KT, S],), kT=([P, KT, S],), v=([P, TT, D],), szT=([P, KT, S],),
                       F=([FH, S],), FR=([P, 2, S],), cm=([P, P],), sums=([P, 4 * FH],), gains=([P, 8],),
                       st=([P, 3, 4],))
            e = mraw[:].rearrange("p a b n -> p (a b) n")
            Pb, PT = e[:, 0:2, :], e[:, 2:4, :]
            pb = lambda u: ajunk if u % 3 == 2 else Pb[:, u % 3, :]
            spread = hT_hi[0:2 * FH, 0:4, :].rearrange("p k s -> p (k s)")
            nh = norm_heads(Group(sq=0, sum=0, root=0, rows=0, nrm=0), 2 * NP, 2, 4, (4, 7), r.sums,
                            lambda n: Pb[:, n % 2, :], lambda n: (r.qT, r.kT)[n % 2][:, n // 2, :],
                            lambda n: r.gains[:, n % 2:n % 2 + 1], (PT[:, 0, :], hT_hi[:, 7, :], hT_lo[:, 7, :]),
                            lambda n: spread[:, P * n:P * (n + 1)])
            q.xn = region(f"fox{j}x", xn=([P, TT, D],)).xn
            w = io["fox_w_in"][j]
            wb = project(w, [c * BW for c in range(8)])
            ob = project(io["fox_w_out"][j], [0, BW], out=True)
            f_small = w.rearrange("(k p) n -> p k n", p=P)[:, :, 4 * D:4 * D + FH]
            units = [(h, t) for h in range(FH) for t in range(TT)]

            def load():
                sp = nc.sync
                small_load(1, f_small, FH)
                for n in range(wb[0].first, wb[-1].last + 1):
                    sp_chunk(n)
                    if n == wb[0].first + 1:
                        sp.wait_ge(*q.region_free)
                        for c, name in ((0, "fox_g_q"), (1, "fox_g_k")):
                            for h in range(2):
                                sp.dma_start(r.gains[h * FD:(h + 1) * FD, c:c + 1],
                                             io[name][j:j + 1].rearrange("a d -> d a")).then_inc(q.cols, 16)
                        sp.dma_start(r.gains[0:FH, 2:3], io["fox_b_f"][j:j + 1].rearrange("a d -> d a")).then_inc(q.cols, 16)
                for n in range(ob[0].first, ob[-1].last + 1):
                    sp_chunk(n)

            def pe():
                t_ = nc.tensor
                pre_pe(q, [])
                for n, b in enumerate(wb):
                    pe_block(b, tok_forms(b) if n in (4, 5) else T_forms(b), hT_hi, hT_lo,
                             q.split_ready if n == 0 else None)
                t_.wait_ge(ps_evac, wb[-1].ev)
                small_project(1, FH)
                if i + 1 < DEPTH:
                    pe_mod(i + 1, (3, 5, 6))
                t_.wait_ge(q.bones, 1)
                nh.pe()
                t_.wait_ge(q.cm, 1)
                t_.wait_ge(q.F_done, 1)
                if i + 1 < DEPTH:
                    t_.wait_ge(G_done, i + 2)

                def decay_row(h):
                    if h >= 1:
                        t_.wait_ge(q.FR, h)
                    else:
                        t_.wait_ge(q.nrm, 2 * NP)
                    t_.matmul(PS[:, 7, :], ident[0:FH, h:h + 1].to_broadcast([FH, P]), r.F[:], start=True, stop=True).then_inc(q.FRm, 1)

                def scores(u):
                    h, t = units[u]
                    if t == 0:
                        decay_row(h)
                    rows = slice(FD * (h % 2), FD * (h % 2) + FD)
                    if u == 0:
                        t_.wait_ge(q.nrm, 2 * NP)
                    if u >= 3:
                        t_.wait_ge(q.ttr, u - 2)
                    n = (t + 1) * P
                    o = PS[:, u % 3, 0:n]
                    t_.matmul(o, r.qT[rows, h // 2, t * P:n], r.kT[rows, h // 2, 0:n], start=True, stop=False)
                    t_.matmul(PS[:, u % 3, t * P:n], ident[:], r.cm[:], start=False, stop=True).then_inc(q.sc, 1)

                def turn(u):
                    h, t = units[u]
                    t_.wait_ge(q.scl, u + 1)
                    if u >= 2:
                        t_.wait_ge(q.pts, u - 1)
                    for k in range(t + 1):
                        mm = t_.transpose(PS[:, 3 + u % 2, k * P:(k + 1) * P], pb(u)[:, k * P:(k + 1) * P], ident[:])
                    mm.then_inc(q.pt, 1)

                def values(u):
                    h, t = units[u]
                    t_.wait_ge(q.pts, u + 1)
                    if h % 2 == 0 and t == 0 and h >= 4:
                        t_.wait_ge(q.os, h // 2 - 1)
                    rows = slice(FD * (h % 2), FD * (h % 2) + FD)
                    for k in range(t + 1):
                        mm = t_.matmul(PS[rows, 5 + (h // 2) % 2, t * P:(t + 1) * P], r.v[:, k, h * FD:(h + 1) * FD],
                                       PT[:, u % 2, k * P:(k + 1) * P], start=k == 0, stop=k == t)
                    mm.then_inc(q.pv, 1)

                scores(0)
                for u in range(len(units) + 2):
                    if u + 1 < len(units):
                        scores(u + 1)
                    if 1 <= u <= len(units):
                        turn(u - 1)
                    if u >= 2:
                        values(u - 2)
                t_.wait_ge(q.os, KT)
                for b in ob:
                    pe_block(b, tok_forms(b), hT_hi, hT_lo)

            def act():
                a = nc.scalar
                pre_act(q, xw, modc[:, i % 2, 0, :], modc[:, i % 2, 1, :], ready=(modc_done, i + 1))
                for n, b in enumerate(wb):
                    split_ahead(act_chunk, b)
                    a.wait_ge(w_used, b.last + 1)
                    src = PS[:, bank_set(b):bank_set(b) + 4, :]
                    if n < 4:
                        a.activation((r.qT, r.kT)[n // 2][:, 4 * (n % 2):4 * (n % 2) + 4, :], src, ACT.Copy).then_inc(ps_evac, 1)
                    elif n < 6:
                        a.activation(r.v[:, :, (n - 4) * BW:(n - 3) * BW], src, ACT.Copy).then_inc(ps_evac, 1)
                    else:
                        a.activation(r.szT[:, 4 * (n - 6):4 * (n - 5), :], src, ACT.Silu).then_inc(ps_evac, 1)
                a.wait_ge(ps_evac, wb[-1].ev)
                if i + 1 < DEPTH:
                    a.wait_ge(m_used, NMC * (i + 2))
                a.wait_ge(small.mm, 2)
                a.wait_ge(q.cols, 80)
                z, bf = r.FR[0:FH, 0, :], r.gains[0:FH, 2:3]
                then_act(a.activation(z, PS[0:FH, 1, :], ACT.Abs, bias=bf))
                then_act(a.activation(z, z, ACT.Exp, scale=-1.0))
                a.activation(z, z, ACT.Ln, bias=1.0).then_inc(q.lz, 1)
                nh.act(lambda n: (r.qT, r.kT)[n % 2][:, n // 2, :])

                def evac(u):
                    h, t = units[u]
                    a.wait_ge(q.pt, u + 1)
                    if u >= 2:
                        a.wait_ge(q.pv, u - 1)
                    a.activation(PT[:, u % 2, 0:(t + 1) * P], PS[:, 3 + u % 2, 0:(t + 1) * P], ACT.Copy).then_inc(q.pts, 1)

                def decay(h):
                    a.wait_ge(q.FRm, h + 1)
                    if h >= 2:
                        a.wait_ge(q.ttr, TT * (h - 1))
                    if h == 0:
                        a.wait_ge(q.nrm, 2 * NP)
                    a.activation(r.FR[:, h % 2, :], PS[:, 7, :], ACT.Copy).then_inc(q.FR, 1)

                decay(0)
                for u, (h, t) in enumerate(units):
                    if t == TT - 1 and h + 1 < FH:
                        decay(h + 1)
                    a.wait_ge(q.ttr, u + 1)
                    p = pb(u)[:, 0:(t + 1) * P]
                    a.activation(p, p, ACT.Exp, scale=-1.0, bias=r.st[:, u % 3, 0:1], accum_out=r.st[:, u % 3, 1:2]).then_inc(q.ex, 1)
                    if u >= 1:
                        evac(u - 1)
                evac(len(units) - 1)
                post_act(q, ob)

            def pool():
                p = nc.gpsimd
                if i + 1 < DEPTH:
                    pool_mod(i + 1)
                p.wait_ge(*q.region_free)
                then_pool(p.memset(r.cm[:], 0.0))
                p.affine_select(out=r.cm[:], in_=r.cm[:], compare_op=ALU.is_ge, fill=NEG, base=0,
                                pattern=[[-1, P]], channel_multiplier=1).then_inc(q.cm, 1)
                then_pool(p.memset(r.sums[:], 0.0))
                for e in range(2):
                    ins = p.memset(r.sums[64 * e:64 * e + 64, 2 * FH + e:2 * FH + e + 1], 1.0)
                ins.then_inc(q.bones, 1)

            def dve():
                v = nc.vector
                pre_dve(q, hT_hi, hT_lo)
                small_dve(1, FH)
                for m, b in enumerate(wb):
                    split_ahead(dve_chunk, b)
                    if i + 1 < DEPTH and m < MB:
                        dve_mod(i + 1, m)
                if i + 1 < DEPTH:
                    dve_modfin(i + 1, (3, 5, 6))
                v.wait_ge(small.mm, 2)
                then_dve(v.tensor_copy(spread.rearrange("p (h d) -> p h d", d=FD),
                                       ident[0:2 * FH, 0:2 * FH].unsqueeze(2).to_broadcast([2 * FH, 2 * FH, FD])))
                v.wait_ge(q.cols, 80)
                v.tensor_scalar(r.gains[:, 0:1], r.gains[:, 0:1], float(FD) ** -0.5, None, ALU.mult)
                v.wait_ge(q.lz, 1)
                then_dve(v.tensor_scalar(r.F[:], PS[0:FH, 1, :], r.gains[0:FH, 2:3], 0.0, ALU.add, ALU.min))
                then_dve(v.tensor_tensor(r.F[:], r.FR[0:FH, 0, :], r.F[:], ALU.subtract))
                v.memset(r.FR[0:FH, 1, :], 1.0).then_inc(q.f1, 1)
                v.wait_ge(q.f1, 1)
                v.tensor_tensor_scan(r.F[:], r.FR[0:FH, 1, :], r.F[:], 0.0, ALU.mult, ALU.add).then_inc(q.F_done, 1)
                nh.dve()

                def scale(u):
                    h, t = units[u]
                    v.wait_ge(q.ex, u + 1)
                    then_dve(v.reciprocal(r.st[:, u % 3, 2:3], r.st[:, u % 3, 1:2]))
                    p = pb(u)[:, 0:(t + 1) * P]
                    v.tensor_scalar(p, p, r.st[:, u % 3, 2:3], None, ALU.mult).then_inc(q.scl, 1)
                    if t == TT - 1 and h % 2 and h >= 3:
                        gate(h // 2 - 1)

                def gate(k):
                    v.wait_ge(q.pv, 2 * TT * (k + 1))
                    then_dve(v.tensor_tensor(hf[:, k % 2, :], PS[:, 5 + k % 2, :], r.szT[:, k, :], ALU.mult))
                    then_dve(v.tensor_copy(hT_hi[:, k, :], hf[:, k % 2, :]))
                    v.tensor_tensor(hT_lo[:, k, :], hf[:, k % 2, :], hT_hi[:, k, :].bitcast(F32), ALU.subtract).then_inc(q.os, 1)

                for u, (h, t) in enumerate(units):
                    n = (t + 1) * P
                    v.wait_ge(q.sc, u + 1)
                    if t == 0:
                        v.wait_ge(q.FR, h + 1)
                    if u >= 3:
                        v.wait_ge(q.pt, u - 2)
                    v.tensor_tensor_reduce(out=pb(u)[:, 0:n], in0=PS[:, u % 3, 0:n], in1=r.FR[:, h % 2, 0:n], scale=-1.0,
                                           scalar=-NEG, op0=ALU.add, op1=ALU.min, accum_out=r.st[:, u % 3, 0:1]).then_inc(q.ttr, 1)
                    if u >= 1:
                        scale(u - 1)
                scale(len(units) - 1)
                gate(NP - 1)
                post_dve(q, ob, G[:, i % 2, :], (G_done, i + 1), None)

            return Group(load=load, pe=pe, act=act, pool=pool, dve=dve)

        grow = Group(landed=sem("grow_landed"))
        mem_x = sig("mem", "landed sq sd xnd tr hf split")

        def pool_gain(l, src):
            if l > DEPTH:
                nc.gpsimd.wait_ge(x_done, TT * l)
            else:
                nc.gpsimd.wait_ge(x_done, TT * DEPTH)
            nc.gpsimd.dma_start(grow.row[:], bass.AP(src.tensor, src.offset, [[0, P], [1, D]])).then_inc(grow.landed, 16)

        def mem_norm(m, raw, xn):
            q = Group(pre=mem_x, tb=2 * m, kb=KT * m, xn=xn, st=stat, raw=raw, late=None)
            return q

        NAT = lambda a, t: a[:, t * P:(t + 1) * P]
        BY4 = lambda a, t: a.rearrange("p (n r) -> p r n", r=4)[:, t, :]
        ORDER = (NAT, BY4, BY4)
        STRIDE = (1, 4, 4)

        su = sig("su", "sc ttr ex scl pt pts pv po")

        def softmax_units(units, u0, s0, p0, buf):
            Pb, PT, st = buf.P, buf.PT, buf.st
            for u, w in enumerate(units):
                w.u, w.norm_n = u0 + u, s0 + sum(z.norm for z in units[:u + 1])
                w.pair = p0 + w.local_pair

            def pe(gate):
                t_ = nc.tensor

                def scores(w):
                    if w.u >= 3:
                        t_.wait_ge(su.ttr, w.u - 2)
                    t_.matmul(PS[:, w.u % 3, 0:w.n], w.q, w.k, start=True, stop=True).then_inc(su.sc, 1)

                def turn(w):
                    t_.wait_ge(*((su.scl, w.norm_n) if w.norm else (su.ex, w.u + 1)))
                    if w.u >= 2:
                        t_.wait_ge(su.pts, w.u - 1)
                    for k in range(w.n // P):
                        mm = t_.transpose(PS[:, 3 + w.u % 2, k * P:(k + 1) * P], Pb[:, w.u % 3, k * P:(k + 1) * P], ident[:])
                    mm.then_inc(su.pt, 1)

                def values(w):
                    t_.wait_ge(su.pts, w.u + 1)
                    if w.first and w.pair >= 2:
                        t_.wait_ge(su.po, w.pair - 1)
                    nk = w.n // P
                    for k in range(nk):
                        mm = t_.matmul(PS[w.rows, 5 + w.pair % 2, w.t * P:(w.t + 1) * P], w.v[k],
                                       PT[:, w.u % 2, k * P:(k + 1) * P], start=k == 0, stop=k == nk - 1)
                    mm.then_inc(su.pv, 1)

                for s in gate:
                    t_.wait_ge(*s)
                scores(units[0])
                for u in range(len(units) + 2):
                    if u + 1 < len(units):
                        scores(units[u + 1])
                    if 1 <= u <= len(units):
                        turn(units[u - 1])
                    if u >= 2:
                        values(units[u - 2])

            def act(out_view):
                a = nc.scalar

                def evac(w):
                    a.wait_ge(su.pt, w.u + 1)
                    if w.u >= 2:
                        a.wait_ge(su.pv, w.u - 1)
                    a.activation(PT[:, w.u % 2, 0:w.n], PS[:, 3 + w.u % 2, 0:w.n], ACT.Copy).then_inc(su.pts, 1)

                def take(w):
                    a.wait_ge(su.pv, w.u + 1)
                    dst, src = out_view(w, PS[:, 5 + w.pair % 2, :])
                    a.activation(dst, src, ACT.Copy).then_inc(su.po, 1)

                for u, w in enumerate(units):
                    a.wait_ge(su.ttr, w.u + 1)
                    p = Pb[:, w.u % 3, 0:w.n]
                    a.activation(p, p, ACT.Exp, scale=-1.0, bias=w.nm, accum_out=w.den).then_inc(su.ex, 1)
                    if u >= 1:
                        evac(units[u - 1])
                    if u >= 2 and units[u - 2].last:
                        take(units[u - 2])
                evac(units[-1])
                if units[-2].last:
                    take(units[-2])
                take(units[-1])

            def dve():
                v = nc.vector

                def scale(w):
                    if not w.norm:
                        return
                    v.wait_ge(su.ex, w.u + 1)
                    then_dve(v.reciprocal(w.rd, w.den))
                    p = Pb[:, w.u % 3, 0:w.n]
                    v.tensor_scalar(p, p, w.rd, None, ALU.mult).then_inc(su.scl, 1)

                for u, w in enumerate(units):
                    v.wait_ge(su.sc, w.u + 1)
                    if w.u >= 3:
                        v.wait_ge(su.pt, w.u - 2)
                    v.tensor_tensor_reduce(out=Pb[:, w.u % 3, 0:w.n], in0=PS[:, w.u % 3, 0:w.n], in1=w.bias, scale=-1.0,
                                           scalar=-NEG, op0=ALU.add, op1=ALU.min, accum_out=w.nm).then_inc(su.ttr, 1)
                    if u >= 1:
                        scale(units[u - 1])
                scale(units[-1])

            return Group(pe=pe, act=act, dve=dve)

        def memory_units(r):
            units = []
            for h in range(MH):
                rows = slice(MD * (h % 2), MD * (h % 2) + MD)
                for t in range(TT):
                    s = (h * TT + t) % 4
                    units.append(Group(
                        q=r.qm[rows, h // 2, t * P:(t + 1) * P], k=r.mk[rows, h // 2, :], n=ML, bias=r.zero[:], norm=True,
                        v=[r.mv[:, k, h * MD:(h + 1) * MD] for k in range(ML // P)], rows=rows, t=t, local_pair=h // 2,
                        first=h % 2 == 0 and t == 0, last=h % 2 == 1 and t == TT - 1, g=3,
                        nm=r.mst[:, s, 0:1], den=r.mst[:, s, 1:2], rd=r.mst[:, s, 2:3]))
            return units

        scr = [nc.dram_tensor(f"band{s}", (P, 512), F32, kind="Internal").ap() for s in range(AH)]

        att_s = sig("att", "tab bandm bands bandw0 bandw1 toe rt wrow e1 e2 wg wb os ready")

        def att_layer(l, xw):
            q = Group(att_s)
            q.st = stat
            norm_front(q, l)
            r = region("att", qk=([P, 12, S],), v=([P, TT, 3 * AHG * 64],), qm=([P, 2, S],), mk=([P, 2, ML],),
                       mv=([P, 2, ML],), B0=([P, AHG, 3 * P],), B1=([P, AHG, P],), B2=([P, AHG, P],), zero=([P, ML],),
                       oT=([P, KT, S],), P=([P, 3, 3 * P],), PT=([P, 2, 3 * P],), nm=([P, AH, TT],), den=([P, AH, TT],),
                       mst=([P, 4, 4],), mhi=([P, KT, ML], F32R), mlo=([P, KT, ML], F32R))
            r.st = None
            q.xn = region("attx", xn=([P, TT, D],)).xn
            mem_raw = r.oT[:, 0:4, :].rearrange("p (t a) s -> p t (a s)", t=2)
            mem_n = r.oT[:, 4:8, :].rearrange("p (t a) s -> p t (a s)", t=2)
            mq = mem_norm(0, mem_raw, mem_n)
            w = io["att_w_in_2"][0]
            wb = project(w, [0, BW, 2 * BW]) + [add_block(w, [(0, 3 * BW + 256 * c, 256)]) for c in range(4)]
            kv = add_block(io["mem_w_kv_2"][0], [(0, 0, BW)])
            ob = project(io["att_w_out_2"][0], [0, BW], out=True)
            tabs = r.qm[0:33, :, :]
            table = r.P[0:33, 0, 0:AH]
            band = r.v[:].rearrange("p t n -> p (t n)")[:, 0:2 * 512].rearrange("p (s n) -> p s n", s=2)

            def load():
                sp = nc.sync
                for n in range(wb[0].first, kv.last + 1):
                    sp_chunk(n)
                for n in range(ob[0].first, ob[-1].last + 1):
                    sp_chunk(n)

            units = []
            for h in range(AH):
                g, hh = h // AHG, h % AHG
                rows = slice(64 * (h % 2), 64 * (h % 2) + 64)
                for t in range(TT):
                    if g == 0:
                        lo, hi = max(t - 1, 0), min(t + 2, TT)
                        k = r.qk[rows, 6 + h // 2, lo * P:hi * P]
                        bias = r.B0[:, hh, (lo - t + 1) * P:(hi - t + 1) * P]
                        tiles = range(lo, hi)
                    else:
                        k = ORDER[g](r.qk[rows, 6 + h // 2, :], t)
                        bias = (r.B1, r.B2)[g - 1][:, hh, :]
                        tiles = (t,)
                    units.append(Group(
                        q=ORDER[g](r.qk[rows, h // 2, :], t), k=k, n=len(tiles) * P, bias=bias, norm=False,
                        v=[r.v[:, kt, h * 64:(h + 1) * 64] for kt in tiles], rows=rows, t=t, local_pair=h // 2,
                        first=h % 2 == 0 and t == 0, last=h % 2 == 1 and t == TT - 1, g=g,
                        nm=r.nm[:, h, t:t + 1], den=r.den[:, h, t:t + 1], rd=None))
            main = softmax_units(units, 0, 0, 0, Group(P=r.P, PT=r.PT, st=None))
            mu = memory_units(r)
            mem = softmax_units(mu, len(units), 0, AH // 2, Group(P=r.P, PT=r.PT, st=None))
            Rn, Rd, Re = (r.qk[0:AHG, 3 * n:3 * n + 3, :] for n in range(3))

            def back(a, g):
                r_ = STRIDE[g]
                return a if g == 0 else a.rearrange("p (r n) -> p r n", r=r_)

            def natural(a, g):
                r_ = STRIDE[g]
                return a if g == 0 else a.rearrange("p (n r) -> p r n", r=r_)

            def pe():
                t_ = nc.tensor
                pre_pe(q, [])
                for h in range(AH):
                    t_.wait_ge(q.tab, 16 * (3 + (h >= 2 * AHG)))
                    if h == 0:
                        t_.wait_ge(q.ready, 1)
                        t_.wait_ge(pre_x.hf, q.kb + KT)
                    if h >= 2:
                        t_.wait_ge(q.bands, h - 1)
                    t_.matmul(PS[:, h % 2, :], table[:, h:h + 1].to_broadcast([33, P]), tabs[:, h // AHG % 2, :],
                              start=True, stop=True).then_inc(q.bandm, 1)
                t_.wait_ge(q.bands, AH)
                for n, b in enumerate(wb):
                    s = bank_set(b)
                    if n < 3:
                        forms = T_forms(b)
                    elif n < 6:
                        forms = [("tok", s + t, ORDER[n - 3], t, 0, 256) for t in range(TT)]
                    else:
                        forms = [("T", s + j, j * P) for j in range(2)]
                    pe_block(b, forms, hT_hi, hT_lo, q.split_ready if n == 0 else None)
                pre_pe(mq, [(ps_evac, wb[-1].ev)], nt=2)
                s = bank_set(kv)
                t_.wait_ge(mem_x.hf, KT)
                pe_block(kv, [("T", s, 0), ("T", s + 1, P), ("tok", s + 2, NAT, 0, 256, 256), ("tok", s + 3, NAT, 1, 256, 256)],
                         r.mhi, r.mlo, {0: (mem_x.split, CK), 1: (mem_x.split, KT)})
                main.pe([(ps_evac, kv.ev), (q.toe, 16 * AH)])
                mem.pe([(q.ready, 2)])
                t_.wait_ge(su.po, AH // 2 + 2)
                for g in range(3):
                    for c, a in ((0, r.nm), (1, r.den)):
                        for t in range(TT):
                            mm = t_.transpose(PS[0:AHG, 3 * c + g, t * P:(t + 1) * P], a[:, g * AHG:(g + 1) * AHG, t], ident[:])
                mm.then_inc(q.rt, 1)
                t_.wait_ge(q.wg, 1)
                for n in range(AH // 2):
                    if n >= 2:
                        t_.wait_ge(q.wb, n - 1)
                    for e in range(2):
                        sel = ident[0:AHG, 2 * (n % 2) + e:2 * (n % 2) + e + 1].to_broadcast([AHG, 64])
                        mm = t_.matmul(PS[64 * e:64 * e + 64, 6 + n % 2, :], sel, Re[:, n // 2, :], start=True, stop=True)
                    mm.then_inc(q.wrow, 1)
                t_.wait_ge(q.os, KT)
                for b in ob:
                    pe_block(b, tok_forms(b), hT_hi, hT_lo)

            def act():
                a = nc.scalar
                pre_act(q, xw, vcol("mix_pre"), None)
                for h in range(AH):
                    a.wait_ge(q.bandm, h + 1)
                    if h >= 2:
                        a.wait_ge((q.bandw0, q.bandw1)[h % 2], 16 * (h // 2))
                    a.activation(band[:, h % 2, :], PS[:, h % 2, :], ACT.Copy).then_inc(q.bands, 1)
                    a.wait_ge(q.bands, h + 1)
                    a.dma_start(scr[h][:, :], band[:, h % 2, :]).then_inc((q.bandw0, q.bandw1)[h % 2], 16)
                a.wait_ge(q.bandw0, 8 * AH)
                a.wait_ge(q.bandw1, 8 * AH)
                for h in range(AH):
                    g, hh = h // AHG, h % AHG
                    dst = (r.B0, r.B1, r.B2)[g][:, hh, :]
                    off = 127 if g == 0 else 255
                    n = 3 * P if g == 0 else P
                    a.dma_start(dst, bass.AP(scr[h].tensor, off, [[511, P], [1, n]])).then_inc(q.toe, 16)
                for n, b in enumerate(wb):
                    split_ahead(act_chunk, b)
                    a.wait_ge(w_used, b.last + 1)
                    s = bank_set(b)
                    if n < 3:
                        if n == 1:
                            a.activation(r.qk[:, 4:6, :], PS[:, s:s + 2, :], ACT.Copy, scale=0.125)
                            a.activation(r.qk[:, 6:8, :], PS[:, s + 2:s + 4, :], ACT.Copy).then_inc(ps_evac, 1)
                        else:
                            a.activation(r.qk[:, 4 * n:4 * n + 4, :], PS[:, s:s + 4, :], ACT.Copy,
                                         scale=0.125 if n == 0 else 1.0).then_inc(ps_evac, 1)
                    elif n < 6:
                        a.activation(r.v[:, :, (n - 3) * 256:(n - 2) * 256], PS[:, s:s + 4, 0:256], ACT.Copy).then_inc(ps_evac, 1)
                    else:
                        a.activation(r.qm[:], PS[:, s:s + 2, :], ACT.Copy, scale=0.125).then_inc(ps_evac, 1)
                pre_act(mq, lambda t: (mem_x.landed, 16), vcol("mem_norm"), None, src=mem_raw, nt=2)
                split_ahead(act_chunk, kv)
                a.wait_ge(w_used, kv.last + 1)
                s = bank_set(kv)
                a.activation(r.mk[:], PS[:, s:s + 2, 0:ML], ACT.Copy)
                a.activation(r.mv[:], PS[:, s + 2:s + 4, 0:ML], ACT.Copy).then_inc(ps_evac, 1)

                def view(w, src):
                    return natural(r.oT[:, w.local_pair + (6 if w.g == 3 else 0), :], w.g % 3), back(src, w.g % 3)

                main.act(view)
                mem.act(view)
                a.wait_ge(q.e1, 1)
                a.activation(Re[:], Rn[:], ACT.Exp, scale=-1.0).then_inc(q.e2, 1)
                post_act(q, ob)

            def pool():
                p = nc.gpsimd
                pool_gain(l, io["norm_mix_post_2"][0:1])
                p.wait_ge(*q.region_free)
                then_pool(p.memset(table, 1.0))
                p.dma_start(table[0:NBUCKET, :], io["rel_bias_2"]).then_inc(q.tab, 16)
                p.dma_start(tabs[:, 0, :], io["rel_onehot"][0]).then_inc(q.tab, 16)
                p.dma_start(tabs[:, 1, :], io["rel_onehot"][1]).then_inc(q.tab, 16)
                p.memset(r.zero[:], 0.0).then_inc(q.ready, 1)
                p.wait_ge(q.bandm, AHG)
                p.dma_start(tabs[:, 0, :], io["rel_onehot"][2]).then_inc(q.tab, 16)
                p.wait_ge(q.tab, 48)
                p.dma_start(mem_raw, io["mem_2"].rearrange("a (t p) d -> p (a t) d", p=P)).then_inc(mem_x.landed, 16)
                p.memset(r.mst[:], 0.0).then_inc(q.ready, 1)

            def dve():
                v = nc.vector
                pre_dve(q, hT_hi, hT_lo)
                for b in wb:
                    split_ahead(dve_chunk, b)
                pre_dve(mq, r.mhi, r.mlo, src=mem_raw, nt=2)
                split_ahead(dve_chunk, kv)
                v.wait_ge(q.toe, 16 * AH)
                main.dve()
                mem.dve()
                v.wait_ge(su.po, AH // 2 + 2)
                for n in (6, 7):
                    then_dve(v.tensor_copy(hT_hi[:, n, :], r.oT[:, n, :]))
                    v.tensor_tensor(hT_lo[:, n, :], r.oT[:, n, :], hT_hi[:, n, :].bitcast(F32), ALU.subtract).then_inc(q.os, 1)
                v.wait_ge(q.rt, 1)
                for g in range(3):
                    for c, dst in ((0, Rn), (1, Rd)):
                        ins = v.tensor_copy(natural(dst[:, g, :], g), back(PS[0:AHG, 3 * c + g, :], g))
                then_dve(ins)
                low = Re[:, 0, :]
                then_dve(v.tensor_tensor(low, Rn[:, 0, :], Rn[:, 1, :], ALU.min))
                then_dve(v.tensor_tensor(low, low, Rn[:, 2, :], ALU.min))
                for g in range(3):
                    ins = v.tensor_tensor(Rn[:, g, :], Rn[:, g, :], low, ALU.subtract)
                ins.then_inc(q.e1, 1)
                v.wait_ge(q.e2, 1)
                then_dve(v.tensor_tensor(Rd[:], Rd[:], Re[:], ALU.mult))
                then_dve(v.tensor_tensor(Rd[:, 0, :], Rd[:, 0, :], Rd[:, 1, :], ALU.add))
                then_dve(v.tensor_tensor(Rd[:, 0, :], Rd[:, 0, :], Rd[:, 2, :], ALU.add))
                then_dve(v.reciprocal(Rd[:, 0, :], Rd[:, 0, :]))
                v.tensor_tensor(Re[:], Re[:], Rd[:, 0:1, :].to_broadcast([AHG, 3, S]), ALU.mult).then_inc(q.wg, 1)
                for n in range(6):
                    v.wait_ge(q.wrow, n + 1)
                    v.tensor_tensor(hf[:, n % 2, :], PS[:, 6 + n % 2, :], r.oT[:, n, :], ALU.mult).then_inc(q.wb, 1)
                    v.wait_ge(q.wb, n + 1)
                    then_dve(v.tensor_copy(hT_hi[:, n, :], hf[:, n % 2, :]))
                    v.tensor_tensor(hT_lo[:, n, :], hf[:, n % 2, :], hT_hi[:, n, :].bitcast(F32), ALU.subtract).then_inc(q.os, 1)
                post_dve(q, ob, grow.row[:], (grow.landed, 16 * (l - DEPTH + 1)), None)

            return Group(load=load, pe=pe, act=act, pool=pool, dve=dve)

        ffn_s = sig("ffn", "sg hid")

        def ffn_layer(l, m, xw):
            q = Group(ffn_s)
            q.st = stat
            norm_front(q, l)
            r = region(f"ffn{m}", hi=([P, FT, S], F32R), lo=([P, FT, S], F32R), sg=([P, 2, S],))
            q.xn = region(f"ffn{m}x", xn=([P, TT, D],)).xn
            w = io["ffn_w_gate_up_2"][m]
            wb = [add_block(w, [(0, 256 * c, 256), (256, FF + 256 * c, 256)]) for c in range(FF // 256)]
            ob = project(io["ffn_w_down_2"][m], [0, BW], out=True)
            NB = len(wb)

            def load():
                for n in range(wb[0].first, ob[-1].last + 1):
                    sp_chunk(n)

            def pe():
                pre_pe(q, [])
                for n, b in enumerate(wb):
                    pe_block(b, T_forms(b), hT_hi, hT_lo, q.split_ready if n == 0 else None)
                nc.tensor.wait_ge(ps_evac, wb[-1].ev)
                for b in ob:
                    pe_block(b, tok_forms(b), r.hi, r.lo, {0: (q.hid, NB * (m + 1))})

            def act():
                a = nc.scalar
                pre_act(q, xw, vcol("ffn_pre", KT * m), None)
                for n, b in enumerate(wb):
                    split_ahead(act_chunk, b)
                    a.wait_ge(w_used, b.last + 1)
                    if n:
                        a.wait_ge(ps_evac, wb[n - 1].ev)
                    s = bank_set(b)
                    a.activation(r.sg[:], PS[:, s:s + 2, :], ACT.Silu).then_inc(q.sg, 1)
                post_act(q, ob)

            def pool():
                pool_gain(l, io["norm_ffn_post_2"][m:m + 1])

            def dve():
                v = nc.vector
                pre_dve(q, hT_hi, hT_lo)
                for n, b in enumerate(wb):
                    split_ahead(dve_chunk, b)
                    v.wait_ge(q.sg, NB * m + n + 1)
                    s = bank_set(b)
                    if m + n:
                        v.wait_ge(q.hid, NB * m + n)
                    v.tensor_tensor(hf[:], r.sg[:], PS[:, s + 2:s + 4, :], ALU.mult).then_inc(ps_evac, 1)
                    v.wait_ge(ps_evac, b.ev)
                    hi = r.hi[:, 2 * n:2 * n + 2, :]
                    then_dve(v.tensor_copy(hi, hf[:]))
                    v.tensor_tensor(r.lo[:, 2 * n:2 * n + 2, :], hf[:], hi.bitcast(F32), ALU.subtract).then_inc(q.hid, 1)
                post_dve(q, ob, grow.row[:], (grow.landed, 16 * (l - DEPTH + 1)), None)

            return Group(load=load, pe=pe, act=act, pool=pool, dve=dve)

        def overlays(stack, common, *sets):
            e = ExitStack()
            make = lambda e, shapes: {n: e.enter_context(nc.sbuf_tensor(f"{stack}_{n}", v[0], v[1] if len(v) > 1 else F32))
                                      for n, v in shapes.items()}
            out = [Group(**make(e, common))]
            for shapes in sets:
                with ExitStack() as e2:
                    out.append(Group(**make(e2, shapes)))
            e.close()
            return out

        def dn_layer(l, xw):
            q = sig("dn", "conv gdve gact gcol mask gr prep eg D Dx nt at "
                    "vte qg ti head root")
            q.nrm = lens.nrm
            B = Group(xm=FH * TT, pc=FH * TT, xe=FH * TT, te=FH * TT, tm=FH * TT, ym=FH * TT, ve=FH, sd=FH * TT,
                                rm=FH, vm=AH, sm=AH // 2, rr=AH // 2, os=KT, kte=AH)
            q.xm, q.pc, q.xe, q.te, q.tm, q.ym = fox_s.sc, fox_s.ttr, fox_s.ex, fox_s.pts, fox_s.pt, fox_s.pv
            q.ve, q.sd, q.rm = fox_s.FR, fox_s.scl, fox_s.FRm
            q.vm, q.sm, q.rr, q.os, q.kte = att_s.bandm, att_s.wrow, att_s.wb, att_s.os, att_s.bands
            q.st = stat
            L0 = 2 * (FH // 2)
            norm_front(q, l)
            HP = NH
            NL = len(LEVELS)
            r, f_, m_, d_ = overlays(
                "dn", dict(qkvT=([P, 3 * HP, S],), szT=([P, HP, S],), oT=([P, 2, S],), low=([P, TT, 24],),
                           par=([P, 2, 12],), z=([P, TT, 12],), g=([P, TT, 12],), beta=([P, TT, 12],), nbeta=([P, TT, 12],),
                           G=([P, 2, TT, NH],), nE=([P, 2, TT, NH],), L=([P, TT, 12],), eL=([P, TT, 12],),
                           kd=([P, TT, 12],), eps=([P, 1],), tri=([P, 2, P],), cm=([P, 2, P],), zr=([P, P], F32R), sums=([P, 4 * NH],)),
                dict(xn=([P, 2, D],), raw=([P, 2, D],)),
                dict(hi=([P, KT, ML], F32R), lo=([P, KT, ML], F32R), qm=([P, 2, S],), mk=([P, 2, ML],), mv=([P, 2, ML],), zero=([P, ML],), P=([P, 3, ML],),
                     PT=([P, 2, ML],), mst=([P, 4, 4],)),
                dict(v=([P, 2, S],), TT=([P, 2, 2, S],), AT=([P, 2, 2, S],), qg=([P, 2, S],), ks=([P, 2, S],),
                     X=([P, 2, S // 2],), S=([P, 2, P],), r=([P, 2, P],), vn=([P, 2, P],), sq=([P, S],)))
            NT = hT_a[:, 6:8, :]
            Tm = hT_b[:, 6:8, :]
            q.xn = region("dnx", xn=([P, TT, D],)).xn
            mem_raw, mem_n = f_.raw[:], f_.xn[:]
            tile = lambda n: r.qkvT[:, HP * (n % 2) + n // 2, :]
            nh = norm_heads(Group(sq=L0, sum=2 * L0, root=1, rows=1, nrm=L0), 2 * NH, 1, 2, (0, 1), r.sums,
                            lambda n: d_.AT[:, 0, n % 2, :], tile, lambda n: 1.0 if n % 2 else float(P) ** -0.5,
                            (d_.TT[:, 0, 0, :], hT_hi[:, 5, :], hT_lo[:, 5, :]),
                            lambda n: identr[0:2 * NH, n:n + 1].to_broadcast([2 * NH, P]))
            gateT = m_.P[0:24, 0:2, :].rearrange("p a s -> p (a s)")
            mq = mem_norm(1, mem_raw, mem_n)
            w = io["dn_w_in_2"][0]
            wb = project(w, [BW * c for c in range(6)]) + [add_block(w, [(0, 3096, 256)])]
            kv = add_block(io["mem_w_kv_2"][1], [(0, 0, BW)])
            ob = project(io["dn_w_out_2"][0], [0, BW], out=True)
            g_small = w.rearrange("(k p) n -> p k n", p=P)[:, :, 3072:3096]
            mu = memory_units(m_)
            mem = softmax_units(mu, 64, 16, 8, Group(P=m_.P, PT=m_.PT, st=None))

            def load():
                small_load(3, g_small, 24)
                for n in range(wb[0].first, ob[-1].last + 1):
                    sp_chunk(n)

            def cs(c):
                return slice(c * P, (c + 1) * P)

            def side(a, lv, d):
                return a.rearrange("p (b h s) -> p b h s", h=2, s=LEVELS[lv])[:, :, d, :]

            def invert_pe(h, lv, hop):
                t_ = nc.tensor
                for d in range(2):
                    i = (NL * h + lv) * 2 + d
                    j = ((NL - 1) * h + lv - 1) * 2 + d
                    if hop == 0:
                        if lv == 0:
                            t_.wait_ge(q.at, 2 * h + 2)
                            t_.wait_ge(q.ti, 2 * h + d + 1)
                        else:
                            t_.wait_ge(q.pc, B.pc + i - 1)
                        for c in range(TT):
                            mm = t_.matmul(PS[:, d, 64 * c:64 * c + 64], NT[:, d, cs(c)],
                                           side(Tm[:, d, cs(c)], lv, d), start=True, stop=True)
                        mm.then_inc(q.xm, 1)
                    elif hop == 1 and lv:
                        t_.wait_ge(q.xe, B.xe + j + 1)
                        t_.wait_ge(q.te, B.te + i - 1)
                        for c in range(TT):
                            mm = t_.matmul(PS[:, d, 256 + 64 * c:256 + 64 * c + 64], d_.TT[:, h % 2, d, cs(c)],
                                           d_.X[:, d, 64 * c:64 * c + 64], start=True, stop=True)
                        mm.then_inc(q.ym, 1)
                    elif hop == 2:
                        t_.wait_ge(q.pc, B.pc + i + 1)
                        if lv == 0:
                            t_.wait_ge(q.Dx, 2 * h + d + 1)
                            t_.wait_ge(q.eg, 2 * h + d + 1)
                        for c in range(TT):
                            mm = t_.transpose(PS[:, 2 + d, cs(c)], Tm[:, d, cs(c)], ident[:])
                        mm.then_inc(q.tm, 1)

            def recur_pe(h, c, hop):
                t_ = nc.tensor
                for d in range(2):
                    cc = cs(c if d == 0 else TT - 1 - c)
                    i = (TT * h + c) * 2 + d
                    j = ((TT - 1) * h + c - 1) * 2 + d
                    if hop == 0:
                        if c == 0 and d == 0:
                            if h:
                                t_.wait_ge(q.os, B.os + h)
                            t_.matmul(PS[:, 6, :], r.zr[0:1, :], r.zr[0:1, 0:1].to_broadcast([1, S]), start=True, stop=False)
                        if c == 1 and d == 0:
                            t_.wait_ge(q.qg, 2 * h + 2)
                        if c:
                            t_.wait_ge(q.sd, B.sd + j + 1)
                            t_.matmul(PS[:, 4 + d, 0:P], r.qkvT[:, HP + h, cc], d_.S[:, d, :], start=True, stop=True).then_inc(q.rm, 1)
                            qg = r.qkvT[:, h, cc] if d == 0 else d_.qg[:, h % 2, cc]
                            t_.matmul(PS[:, 6, cc], d_.S[:, d, :], qg, start=False, stop=False)
                    elif hop == 1:
                        if c:
                            t_.wait_ge(q.rr, B.rr + j + 1)
                        elif d == 0:
                            t_.wait_ge(q.te, B.te + 2 * NL * (h + 1))
                        rhs = d_.r[:, d, :] if c else d_.v[:, h % 2, cc]
                        t_.matmul(PS[:, 4 + d, P:2 * P], d_.TT[:, h % 2, d, cc], rhs, start=True, stop=True).then_inc(q.vm, 1)
                    else:
                        t_.wait_ge(q.ve, B.ve + i + 1)
                        if c < TT - 1:
                            kd = r.qkvT[:, 2 * HP + h, cc] if d == 0 else d_.ks[:, h % 2, cc]
                            t_.matmul(PS[:, 4 + d, 2 * P:3 * P], kd, d_.vn[:, d, :], start=True, stop=True).then_inc(q.sm, 1)
                        mm = t_.matmul(PS[:, 6, cc], d_.vn[:, d, :], d_.AT[:, h % 2, d, cc], start=False, stop=c == TT - 1 and d == 1)
                        if c == TT - 1 and d == 1:
                            mm.then_inc(q.head, 1)

            def pe():
                t_ = nc.tensor
                pre_pe(q, [])
                for n, b in enumerate(wb):
                    forms = T_forms(b) if n < 6 else [("T", bank_set(b) + j, j * P) for j in range(2)]
                    pe_block(b, forms, hT_hi, hT_lo, q.split_ready if n == 0 else None)
                t_.wait_ge(ps_evac, wb[-1].ev)
                small_project(3, 24)
                t_.wait_ge(small.read, 1)
                for t in range(TT):
                    mm = t_.transpose(PS[:, 0, 32 * t:32 * t + 24], gateT[:, t * P:(t + 1) * P], ident[0:24, 0:24])
                mm.then_inc(small.turned, 1)
                pre_pe(mq, [(small.read, 2)], nt=2)
                s = bank_set(kv)
                t_.wait_ge(mem_x.hf, 2 * KT)
                pe_block(kv, [("T", s, 0), ("T", s + 1, P), ("tok", s + 2, NAT, 0, 256, 256), ("tok", s + 3, NAT, 1, 256, 256)],
                         m_.hi, m_.lo, {0: (mem_x.split, KT + CK), 1: (mem_x.split, 2 * KT)})
                t_.wait_ge(ps_evac, kv.ev)
                t_.wait_ge(q.gdve, 3)
                t_.wait_ge(q.mask, 3)
                for d in range(2):
                    t_.matmul(PS[:, 7, 24 * d:24 * d + 24], r.tri[:, d, :], r.g[:, :, NH * d:NH * d + NH], start=True, stop=True)
                t_.matmul(PS[:, 7, 48:96], ones[:], r.g[:], start=True, stop=True).then_inc(q.gcol, 1)
                mem.pe([(q.mask, 1)])
                t_.wait_ge(su.po, 10)
                nh.pe()
                for h in range(NH + 1):
                    if h < NH:
                        t_.wait_ge(q.gdve, 4)
                        t_.wait_ge(q.nrm, L0 + 2 * h + 2)
                        for d in range(2):
                            if h:
                                t_.wait_ge(q.te, B.te + 2 * NL * (h - 1) + 2 * NL - 1 + d)
                            for c in range(TT):
                                mm = t_.matmul(PS[:, 2 + d, cs(c)], r.g[:, c, NH * d + h:NH * d + h + 1].to_broadcast([P, P]),
                                               r.tri[:, d, :], start=True, stop=True)
                            mm.then_inc(q.gr, 1)
                        if h == 0:
                            t_.wait_ge(q.nrm, L0 + 2 * NH)
                        for n, rhs in enumerate((HP + h, h)):
                            for c in range(TT):
                                mm = t_.matmul(PS[:, n, cs(c)], r.qkvT[:, HP + h, cs(c)], r.qkvT[:, rhs, cs(c)], start=True, stop=True)
                            mm.then_inc(q.prep, 1)
                        if h:
                            t_.wait_ge(q.kte, B.kte + h)
                        if h >= 2:
                            t_.wait_ge(q.root, 2 * h - 2)
                        for n in (2 * HP + h, HP + h):
                            if n < 2 * HP:
                                t_.wait_ge(q.vte, h + 1)
                            for c in range(TT):
                                mm = t_.transpose(PS[:, 7, cs(c)], r.qkvT[:, n, cs(c)], ident[:])
                            mm.then_inc(q.prep, 1)
                    for lv in range(NL):
                        for hop in range(3):
                            if h < NH:
                                invert_pe(h, lv, hop)
                            if h and lv < TT:
                                recur_pe(h - 1, lv, hop)
                        if h and lv == TT:
                            t_.wait_ge(q.root, 2 * h - 1)
                            if h < NH:
                                t_.wait_ge(q.kte, B.kte + h + 1)
                            t_.matmul(PS[:, 7, :], ones[:], d_.sq[:], start=True, stop=True).then_inc(q.head, 1)
                t_.wait_ge(q.os, B.os + KT)
                for b in ob:
                    pe_block(b, tok_forms(b), hT_hi, hT_lo)

            def conv_done(n):
                return 20 * (n + 1) if n < 4 else 90

            def act():
                a = nc.scalar
                pre_act(q, xw, vcol("mix_pre", KT), None)
                for n, b in enumerate(wb):
                    split_ahead(act_chunk, b)
                    a.wait_ge(w_used, b.last + 1)
                    s = bank_set(b)
                    if n < 5:
                        a.wait_ge(q.conv, conv_done(n))
                        v = r.qkvT[:, 4 * n:min(4 * n + 4, 3 * HP), :]
                        ins = a.activation(v, v, ACT.Silu)
                        if n < 4:
                            ins.then_inc(ps_evac, 1)
                        else:
                            a.activation(r.szT[:, 0:2, :], PS[:, s + 2:s + 4, :], ACT.Silu).then_inc(ps_evac, 1)
                    elif n == 5:
                        a.activation(r.szT[:, 2:6, :], PS[:, s:s + 4, :], ACT.Silu).then_inc(ps_evac, 1)
                    else:
                        a.activation(m_.qm[:], PS[:, s:s + 2, :], ACT.Copy, scale=0.125).then_inc(ps_evac, 1)
                a.wait_ge(q.gdve, 2)
                beta = r.low[:].rearrange("p t (d k h) -> p t d k h", d=2, k=2)
                a.activation(r.beta[:].rearrange("p t (d h) -> p t d h", d=2), beta[:, :, :, 1, :], ACT.Sigmoid)
                then_act(a.activation(r.g[:], r.z[:], ACT.Abs))
                then_act(a.activation(r.g[:], r.g[:], ACT.Exp, scale=-1.0))
                a.activation(r.par[:, 0, :], r.par[:, 0, :], ACT.Exp)
                a.activation(r.g[:], r.g[:], ACT.Ln, bias=1.0).then_inc(q.gact, 1)
                pre_act(mq, lambda t: (mem_x.landed, 64), vcol("mem_norm", KT), None, src=mem_raw, nt=2)
                split_ahead(act_chunk, kv)
                a.wait_ge(w_used, kv.last + 1)
                s = bank_set(kv)
                a.activation(m_.mk[:], PS[:, s:s + 2, 0:ML], ACT.Copy)
                a.activation(m_.mv[:], PS[:, s + 2:s + 4, 0:ML], ACT.Copy).then_inc(ps_evac, 1)
                a.wait_ge(q.gdve, 4)
                a.activation(r.eL[:], r.L[:], ACT.Exp)
                a.activation(r.nE[:], r.G[:], ACT.Exp)
                a.activation(r.kd[:], r.kd[:], ACT.Exp).then_inc(q.gact, 1)
                mem.act(lambda w, src: (r.oT[:, w.local_pair, :], src))
                a.wait_ge(su.po, 10)
                nh.act(tile)
                for h in range(NH + 1):
                    p = h % 2
                    if h < NH:
                        a.wait_ge(q.prep, 4 * h + 3)
                        a.activation(d_.v[:, p, :], PS[:, 7, :], ACT.Copy).then_inc(q.vte, 1)
                        for d in range(2):
                            a.wait_ge(q.gr, 2 * h + d + 1)
                            a.wait_ge(q.D, 2 * h + d + 1)
                            if d == 0 and h:
                                a.wait_ge(q.qg, 2 * h)
                            e = ajunk[:] if d == 0 else d_.qg[:, p, :]
                            a.activation(e, PS[:, 2 + d, :], ACT.Exp).then_inc(q.eg, 1)
                            D_ = d_.AT[:, p, d, :]
                            a.activation(D_, D_, ACT.Exp).then_inc(q.Dx, 1)
                        a.wait_ge(q.prep, 4 * h + 4)
                        for d in range(2):
                            kd = (r.qkvT[:, 2 * HP + h, :], d_.ks[:, p, :])[d]
                            for c in range(TT):
                                ins = a.activation(kd[:, cs(c)], PS[:, 7, cs(c)], ACT.Identity,
                                                   scale=r.kd[:, c, NH * d + h:NH * d + h + 1])
                        ins.then_inc(q.kte, 1)
                    for lv in range(NL):
                        if h < NH and lv:
                            for d in range(2):
                                i = (NL * h + lv) * 2 + d
                                a.wait_ge(q.xm, B.xm + i + 1)
                                a.activation(d_.X[:, d, :], PS[:, d, 0:256], ACT.Copy).then_inc(q.xe, 1)
                        if h and lv < TT:
                            for d in range(2):
                                c = lv if d == 0 else TT - 1 - lv
                                a.wait_ge(q.vm, B.vm + (TT * (h - 1) + lv) * 2 + d + 1)
                                a.activation(d_.vn[:, d, :], PS[:, 4 + d, P:2 * P], ACT.Identity,
                                             scale=r.beta[:, c, NH * d + h - 1:NH * d + h]).then_inc(q.ve, 1)
                        if h < NH:
                            for d in range(2):
                                i = (NL * h + lv) * 2 + d
                                a.wait_ge(q.tm, B.tm + i + 1)
                                a.activation(d_.TT[:, p, d, :], PS[:, 2 + d, :], ACT.Copy).then_inc(q.te, 1)
                        if h and lv == TT - 1:
                            a.wait_ge(q.head, 2 * h - 1)
                            if h > 1:
                                a.wait_ge(q.os, B.os + h - 1)
                            a.activation(d_.sq[:], PS[:, 6, :], ACT.Square).then_inc(q.root, 1)
                        if h and lv == TT:
                            a.wait_ge(q.head, 2 * h)
                            a.activation(d_.sq[:], PS[:, 7, :], ACT.Sqrt, scale=1.0 / P, bias=r.eps[:]).then_inc(q.root, 1)
                post_act(q, ob)

            def pool():
                p = nc.gpsimd
                pool_gain(l, io["norm_mix_post_2"][1:2])
                p.dma_start(r.par[:, 0, :], bass.AP(io["dn_a_log_2"].tensor, 0, [[0, P], [1, 12]])).then_inc(mem_x.landed, 16)
                p.dma_start(r.par[:, 1, :], bass.AP(io["dn_dt_bias_2"].tensor, 0, [[0, P], [1, 12]])).then_inc(mem_x.landed, 16)
                p.dma_start(mem_raw, io["mem_2"].rearrange("a (t p) d -> p (a t) d", p=P)).then_inc(mem_x.landed, 16)
                p.memset(r.eps[:], EPS)
                p.memset(m_.zero[:], 0.0)
                p.memset(m_.mst[:], 0.0).then_inc(q.mask, 1)
                for d, sgn in ((0, 1), (1, -1)):
                    then_pool(p.memset(r.tri[:, d, :], 1.0))
                    then_pool(p.memset(r.cm[:, d, :], 0.0))
                    p.affine_select(out=r.tri[:, d, :], in_=r.tri[:, d, :], compare_op=ALU.is_ge, fill=0.0, base=0,
                                    pattern=[[sgn, P]], channel_multiplier=-sgn)
                    p.affine_select(out=r.cm[:, d, :], in_=r.cm[:, d, :], compare_op=ALU.is_ge, fill=NEG, base=0,
                                    pattern=[[sgn, P]], channel_multiplier=-sgn).then_inc(q.mask, 1)
                p.wait_ge(su.po, 10)
                for h in range(NH):
                    for d in range(2):
                        if h:
                            p.wait_ge(q.tm, B.tm + 2 * NL * h - 1 + d)
                        p.tensor_copy(Tm[:, d, :].rearrange("p (c s) -> p c s", c=TT),
                                      ident[:].unsqueeze(1).to_broadcast([P, TT, P])).then_inc(q.ti, 1)
                    p.wait_ge(q.eg, 2 * h + 2)
                    p.wait_ge(q.nrm, L0 + 2 * h + 1)
                    p.tensor_tensor(d_.qg[:, h % 2, :], d_.qg[:, h % 2, :], r.qkvT[:, h, :], ALU.mult).then_inc(q.qg, 1)
                    p.wait_ge(q.eg, 2 * h + 1)
                    p.wait_ge(q.prep, 4 * h + 2)
                    p.wait_ge(q.qg, 2 * h + 1)
                    p.tensor_tensor(r.qkvT[:, h, :], ajunk[:], r.qkvT[:, h, :], ALU.mult).then_inc(q.qg, 1)

            def dve():
                v = nc.vector
                pre_dve(q, hT_hi, hT_lo)
                small_dve(3, 24)
                step = 0
                for n, b in enumerate(wb):
                    split_ahead(dve_chunk, b)
                    if n >= 5:
                        continue
                    v.wait_ge(w_used, b.last + 1)
                    tiles = 4 if n < 4 else 2
                    for tap in (2, 0, 1, 3, 4):
                        o = tap - CONV // 2
                        lo, hi = max(0, -o), S - max(0, o)
                        for j in range(tiles):
                            f = 4 * n + j
                            src = PS[:, bank_set(b) + j, lo + o:hi + o]
                            dst = r.qkvT[:, f, lo:hi]
                            wc = conv_cols[:, 3 * HP * tap + f:3 * HP * tap + f + 1]
                            if tap == 2:
                                ins = v.tensor_scalar(dst, src, wc, None, ALU.mult)
                            else:
                                v.wait_ge(q.conv, step - tiles + 1)
                                ins = v.scalar_tensor_tensor(out=dst, in0=src, scalar=wc, in1=dst, op0=ALU.mult, op1=ALU.add)
                            ins.then_inc(q.conv, 1)
                            step += 1
                v.wait_ge(small.mm, 4)
                v.tensor_copy(gateT, PS[0:24, 1, :]).then_inc(small.read, 1)
                v.wait_ge(small.turned, 1)
                v.tensor_copy(r.low[:], PS[:, 0, 0:P].rearrange("p (t c) -> p t c", t=TT)[:, :, 0:24]).then_inc(small.read, 1)
                v.wait_ge(small.read, 2)
                v.wait_ge(mem_x.landed, 64)
                zin = r.low[:].rearrange("p t (d k h) -> p t d k h", d=2, k=2)[:, :, :, 0, :]
                for d in range(2):
                    v.tensor_tensor(r.z[:, :, NH * d:NH * d + NH], r.low[:, :, 12 * d:12 * d + NH],
                                    r.par[:, 1:2, NH * d:NH * d + NH].to_broadcast([P, TT, NH]), ALU.add).then_inc(q.gdve, 1)
                then_dve(v.memset(r.sums[:], 0.0))
                v.memset(r.sums[:, 2 * NH:2 * NH + 1], 1.0)
                v.tensor_scalar(r.zr[:], ident[:], 0.0, None, ALU.mult)
                v.wait_ge(q.gact, 1)
                then_dve(v.scalar_tensor_tensor(out=r.g[:], in0=r.z[:], scalar=0.0, in1=r.g[:], op0=ALU.max, op1=ALU.add))
                v.tensor_scalar(r.nbeta[:], r.beta[:], -1.0, None, ALU.mult)
                v.scalar_tensor_tensor(out=r.g[:], in0=r.g[:], scalar=-1.0, in1=r.par[:, 0:1, :].to_broadcast([P, TT, 12]),
                                       op0=ALU.mult, op1=ALU.mult).then_inc(q.gdve, 1)
                pre_dve(mq, m_.hi, m_.lo, src=mem_raw, nt=2)
                split_ahead(dve_chunk, kv)
                v.wait_ge(q.gcol, 1)
                v.tensor_copy(r.G[:].rearrange("p d t h -> p (d t h)"), PS[:, 7, 0:48])
                then_dve(v.tensor_copy(r.L[:].rearrange("p t h -> p (t h)"), PS[:, 7, 48:96]))
                for d in range(2):
                    ins = v.tensor_tensor(r.kd[:, :, NH * d:NH * d + NH], r.L[:, :, NH * d:NH * d + NH], r.G[:, d, :, :], ALU.subtract)
                ins.then_inc(q.gdve, 1)
                v.wait_ge(q.gact, 2)
                v.tensor_scalar(r.nE[:], r.nE[:], -1.0, None, ALU.mult).then_inc(q.gdve, 1)
                mem.dve()
                nh.dve()
                v.wait_ge(q.gdve, 5)
                for h in range(NH + 1):
                    p = h % 2
                    if h < NH:
                        if h == 0:
                            v.wait_ge(q.nrm, L0 + 2 * NH)
                        for d in range(2):
                            v.wait_ge(q.gr, 2 * h + d + 1)
                            for c in range(TT):
                                ins = v.scalar_tensor_tensor(out=d_.AT[:, p, d, cs(c)], in0=PS[:, 2 + d, cs(c)],
                                                             scalar=r.G[:, d, c, h:h + 1], in1=r.cm[:, d, :],
                                                             op0=ALU.subtract, op1=ALU.add)
                            ins.then_inc(q.D, 1)
                        for d in range(2):
                            v.wait_ge(q.Dx, 2 * h + d + 1)
                            if d == 0:
                                v.wait_ge(q.prep, 4 * h + 1)
                            for c in range(TT):
                                ins = v.scalar_tensor_tensor(out=NT[:, d, cs(c)], in0=PS[:, 0, cs(c)],
                                                             scalar=r.nbeta[:, c, NH * d + h:NH * d + h + 1],
                                                             in1=d_.AT[:, p, d, cs(c)], op0=ALU.mult, op1=ALU.mult)
                            ins.then_inc(q.nt, 1)
                        v.wait_ge(q.prep, 4 * h + 2)
                        for d in range(2):
                            if d == 0:
                                v.wait_ge(q.nt, 2 * h + 2)
                            v.tensor_tensor(d_.AT[:, p, d, :], d_.AT[:, p, d, :], PS[:, 1, :], ALU.mult).then_inc(q.at, 1)
                    for lv in range(NL):
                        if 1 <= lv < TT and h:
                            for d in range(2):
                                c = lv if d == 0 else TT - 1 - lv
                                v.wait_ge(q.rm, B.rm + ((TT - 1) * (h - 1) + lv - 1) * 2 + d + 1)
                                v.scalar_tensor_tensor(out=d_.r[:, d, :], in0=PS[:, 4 + d, 0:P], scalar=r.nE[:, d, c, h - 1:h],
                                                       in1=d_.v[:, 1 - p, cs(c)], op0=ALU.mult, op1=ALU.add).then_inc(q.rr, 1)
                        if h < NH:
                            for d in range(2):
                                i = (NL * h + lv) * 2 + d
                                s = LEVELS[lv]
                                if lv == 0:
                                    v.wait_ge(q.ti, 2 * h + d + 1)
                                    v.wait_ge(q.xm, B.xm + i + 1)
                                else:
                                    v.wait_ge(q.ym, B.ym + ((NL - 1) * h + lv - 1) * 2 + d + 1)
                                    v.wait_ge(q.pc, B.pc + i - 1)
                                    if lv == 1:
                                        v.wait_ge(q.tm, B.tm + i - 1)
                                src = PS[:, d, 256 * (lv > 0):256 * (lv > 0) + 256].rearrange("p (c b s) -> p c b s", c=TT, s=s)
                                dst = Tm[:, d, :].rearrange("p (c b h s) -> p c b h s", c=TT, h=2, s=s)[:, :, :, d, :]
                                mask = lvl[:, (NL + lv) if d == 0 else lv, :].rearrange("p (b h s) -> p b h s", h=2, s=s)[:, :, d, :]
                                v.wait_ge(q.tm, B.tm + i - 1 if i else 0) if i > 1 else None
                                v.copy_predicated(dst, mask.unsqueeze(1).to_broadcast([P, TT, P // (2 * s), s]), src).then_inc(q.pc, 1)
                        if h and lv < TT - 1:
                            for d in range(2):
                                c = lv if d == 0 else TT - 1 - lv
                                j = ((TT - 1) * (h - 1) + lv) * 2 + d
                                v.wait_ge(q.sm, B.sm + j + 1)
                                new = PS[:, 4 + d, 2 * P:3 * P]
                                if lv == 0:
                                    v.tensor_copy(d_.S[:, d, :], new).then_inc(q.sd, 1)
                                else:
                                    v.wait_ge(q.sd, B.sd + j - 1)
                                    v.scalar_tensor_tensor(out=d_.S[:, d, :], in0=d_.S[:, d, :],
                                                           scalar=r.eL[:, c, NH * d + h - 1:NH * d + h], in1=new,
                                                           op0=ALU.mult, op1=ALU.add).then_inc(q.sd, 1)
                        if h and lv == TT + 1:
                            k = h - 1
                            v.wait_ge(q.root, 2 * h)
                            then_dve(v.reciprocal(d_.sq[:], d_.sq[:]))
                            then_dve(v.scalar_tensor_tensor(out=hf[:, 0, :], in0=PS[:, 6, :], scalar=vcol("out_norm", 0, 1),
                                                            in1=d_.sq[:], op0=ALU.mult, op1=ALU.mult))
                            then_dve(v.tensor_tensor(hf[:, 0, :], hf[:, 0, :], r.szT[:, k, :], ALU.mult))
                            then_dve(v.tensor_copy(hT_hi[:, k, :], hf[:, 0, :]))
                            v.tensor_tensor(hT_lo[:, k, :], hf[:, 0, :], hT_hi[:, k, :].bitcast(F32), ALU.subtract).then_inc(q.os, 1)
                            v.wait_ge(q.os, B.os + h)
                v.wait_ge(q.tm, B.tm + 2 * NL * NH)
                for n in range(2):
                    then_dve(v.tensor_copy(hT_hi[:, 6 + n, :], r.oT[:, n, :]))
                    v.tensor_tensor(hT_lo[:, 6 + n, :], r.oT[:, n, :], hT_hi[:, 6 + n, :].bitcast(F32), ALU.subtract).then_inc(q.os, 1)
                post_dve(q, ob, grow.row[:], (grow.landed, 16 * (l - DEPTH + 1)), None)

            return Group(load=load, pe=pe, act=act, pool=pool, dve=dve)

        LAYER = [lambda xw: gla_layer(0, 0, xw), lambda xw: sgu_layer(1, 0, xw), lambda xw: fox_layer(2, 0, xw),
                 lambda xw: gla_layer(3, 1, xw), lambda xw: att_layer(4, xw), lambda xw: ffn_layer(5, 0, xw),
                 lambda xw: dn_layer(6, xw), lambda xw: ffn_layer(7, 1, xw)]

        def after(n):
            return lambda t: (x_done, TT * n + t + 1)

        layers = []
        for n, layer in enumerate(LAYER):
            xw = (lambda t: (x_landed, 16)) if n == 0 else after(n - 1)
            if n == DEPTH:
                first.close()
                grow.row = sb("grow_row", [P, D])
            layers.append(layer(xw))
        landings()
        block = ctx.enter_context(nc.Block())

        @block.sync
        def _(sp):
            sp_setup()
            for l in layers:
                l.load()
            for t in range(TT):
                sp.wait_ge(x_done, TT * (len(layers) - 1) + t + 1)
                sp.dma_start(out.rearrange("a (t p) d -> p (a t) d", p=P)[:, t, :], x[:, t, :]).then_inc(out_done, 16)
            sp.wait_ge(out_done, 16 * TT)

        @block.gpsimd
        def _(pool):
            pool_setup()
            pool_mod(0)
            for l in layers:
                l.pool()

        @block.scalar
        def _(act):
            act_setup()
            act_chunk(0)
            act_chunk(1)
            for l in layers:
                l.act()

        @block.tensor
        def _(pe):
            pe_setup()
            pe_mod(0, (4, 5, 6))
            pe.wait_ge(G_done, 1)
            for l in layers:
                l.pe()

        @block.vector
        def _(dve):
            dve_setup()
            for m in range(MB):
                dve_mod(0, m)
            dve_modfin(0, (4, 5, 6))
            dve_chunk(0)
            dve_chunk(1)
            for l in layers:
                l.dve()


def onehot_tables():
    import numpy as np

    out = np.zeros((len(DILS), NBUCKET + 1, 512), np.float32)
    for g, dil in enumerate(DILS):
        for c in range(512):
            r = c - 255
            step = max(dil // 4, 1)
            if r % step or abs(r // step) > HALF:
                out[g, NBUCKET, c] = NEG
                continue
            rel, half, exact = r // step * dil, NBUCKET // 2, NBUCKET // 4
            n = abs(rel)
            if n >= exact:
                n = min(exact + int(np.log(n / exact) / np.log(MAXDIST / exact) * (half - exact)), half - 1)
            out[g, (rel > 0) * half + n, c] = 1.0
    return out


NAMES = ("x c norm_pre_g norm_post_g w_mod b_mod gla_w_in gla_w_a2 gla_b_a gla_g_head gla_w_out sgu_w_in sgu_ln_g "
         "sgu_ln_b sgu_w_s sgu_b_s sgu_w_out fox_w_in fox_b_f fox_g_q fox_g_k fox_w_out mem_2 rel_bias_2 att_w_in_2 "
         "att_w_out_2 dn_w_in_2 dn_conv_2 dn_a_log_2 dn_dt_bias_2 dn_out_norm_2 dn_w_out_2 mem_norm_2 mem_w_kv_2 "
         "norm_mix_pre_2 norm_mix_post_2 norm_ffn_pre_2 norm_ffn_post_2 ffn_w_gate_up_2 ffn_w_down_2").split()


def kernel(**inputs):
    import numpy as np
    import concourse.bacc as bacc
    from concourse.bass_utils import run_bass_kernel_spmd as run

    nc = bacc.Bacc("TRN2", target_bir_lowering=False, num_devices=1)
    arrays, io = {}, {}
    for name in NAMES:
        a = np.ascontiguousarray(inputs[name])
        arrays[f"in_{name}"] = a
        io[name] = nc.dram_tensor(f"in_{name}", a.shape, mybir.dt.from_np(a.dtype), kind="ExternalInput").ap()
    arrays["rel_onehot"] = onehot_tables()
    io["rel_onehot"] = nc.dram_tensor("rel_onehot", (3, NBUCKET + 1, 512), F32, kind="ExternalInput").ap()
    out = nc.dram_tensor("out_x", (1, S, D), F32, kind="ExternalOutput").ap()
    program(nc, io, out)
    return run(nc, [arrays], core_ids=[0]).results[0]["out_x"]
```
